# Optimizing a Trainium2 kernel written in Bass

```python
import jax, jax.numpy as jnp
from jax import lax
import numpy as np

D_MODEL = 1024
BATCH = 1
SEQ = 256
DEPTH = 2

N_META = 16
N_MIXERS = 2
D_FF = 2816
CONV_WIDTH = 3
GLA_HEADS = 4
GLA_DK = D_MODEL // 2
GLA_DV = D_MODEL
GLA_HEAD_K = GLA_DK // GLA_HEADS
GLA_HEAD_V = GLA_DV // GLA_HEADS
GLA_GATE_RANK = 16
GLA_GATE_NORMALIZER = 16.0
GLA_CHUNK = 64
DEEPNORM_ALPHA = (2.0 * DEPTH) ** 0.25
DEEPNORM_BETA = (8.0 * DEPTH) ** -0.25
LN_EPS = 1e-5
RMS_EPS = 1e-6
N_CONV_LAYERS = (DEPTH + 1) // 2
N_GLA_LAYERS = DEPTH // 2

kernel_name = "hybrid_shortconv_gla_macaron_deepnorm"

def layer_norm(x, gain, bias):
    xf = x.astype(jnp.float32)
    mu = jnp.mean(xf, axis=-1, keepdims=True)
    var = jnp.mean(jnp.square(xf - mu), axis=-1, keepdims=True)
    y = (xf - mu) * lax.rsqrt(var + LN_EPS) * gain.astype(jnp.float32) + bias.astype(jnp.float32)
    return y.astype(x.dtype)

def swiglu_ffn(h, w_in, w_out):
    gate, up = jnp.split(h @ w_in, 2, axis=-1)
    return (jax.nn.silu(gate) * up) @ w_out

def short_conv_mixer(h, w_in, w_conv, w_out):
    bgate, cgate, u = jnp.split(h @ w_in, 3, axis=-1)
    u = cgate * u
    L = u.shape[1]
    up = jnp.pad(u, ((0, 0), (CONV_WIDTH - 1, 0), (0, 0)))
    conv = w_conv[0] * up[:, 0:L]
    for tap in range(1, CONV_WIDTH):
        conv = conv + w_conv[tap] * up[:, tap:tap + L]
    return (bgate * conv) @ w_out

def gla_mixer(h, w_in, w_gate_up, b_gate, norm_w, w_out):
    bsz, L, _ = h.shape
    f32 = jnp.float32
    splits = [GLA_DK, 2 * GLA_DK, 2 * GLA_DK + GLA_DV, 2 * GLA_DK + 2 * GLA_DV]
    q, k, v, g, gz = jnp.split(h @ w_in, splits, axis=-1)
    log_a = jax.nn.log_sigmoid((gz @ w_gate_up + b_gate).astype(f32)) / GLA_GATE_NORMALIZER
    q = q.astype(f32) * (GLA_HEAD_K ** -0.5)
    k = k.astype(f32)
    v = v.astype(f32)
    pad = (-L) % GLA_CHUNK
    padw = ((0, 0), (pad, 0), (0, 0))
    q, k, v, log_a = (jnp.pad(t, padw) for t in (q, k, v, log_a))
    Lp = L + pad
    nc = Lp // GLA_CHUNK

    def to_chunks(t, d):
        return t.reshape(bsz, nc, GLA_CHUNK, GLA_HEADS, d).transpose(1, 0, 3, 2, 4)

    q = to_chunks(q, GLA_HEAD_K)
    k = to_chunks(k, GLA_HEAD_K)
    v = to_chunks(v, GLA_HEAD_V)
    b = jnp.cumsum(to_chunks(log_a, GLA_HEAD_K), axis=3)
    b_ref = b[:, :, :, GLA_CHUNK // 2:GLA_CHUNK // 2 + 1, :]
    b_last = b[:, :, :, -1:, :]
    scores = jnp.einsum('nbhik,nbhjk->nbhij', q * jnp.exp(b - b_ref), k * jnp.exp(b_ref - b))
    causal = jnp.tril(jnp.ones((GLA_CHUNK, GLA_CHUNK), dtype=bool))
    scores = jnp.where(causal, scores, 0.0)
    o_intra = jnp.einsum('nbhij,nbhjv->nbhiv', scores, v)
    q_inter = q * jnp.exp(b)
    k_state = k * jnp.exp(b_last - b)
    decay = jnp.exp(b_last[:, :, :, 0, :])

    def step(state, xs):
        qi, ks, vi, dec = xs
        o = jnp.einsum('bhck,bhkv->bhcv', qi, state)
        state = dec[..., None] * state + jnp.einsum('bhck,bhcv->bhkv', ks, vi)
        return state, o

    s0 = jnp.zeros((bsz, GLA_HEADS, GLA_HEAD_K, GLA_HEAD_V), f32)
    _, o_inter = lax.scan(step, s0, (q_inter, k_state, v, decay))
    o = (o_intra + o_inter).transpose(1, 0, 3, 2, 4).reshape(bsz, Lp, GLA_HEADS, GLA_HEAD_V)[:, pad:]
    o = o * lax.rsqrt(jnp.mean(jnp.square(o), axis=-1, keepdims=True) + RMS_EPS) * norm_w.astype(f32)
    o = o.reshape(bsz, L, GLA_DV).astype(h.dtype) * jax.nn.silu(g)
    return o @ w_out

def setup_inputs(seed: int = 0) -> dict:
    key = jax.random.key(seed)
    ks = jax.random.split(key, 16)
    nrm = jax.random.normal
    D, F = D_MODEL, D_FF
    gla_in_width = 2 * GLA_DK + 2 * GLA_DV + GLA_GATE_RANK
    return {
        "x": nrm(ks[0], (BATCH, SEQ, D), jnp.float32),
        "meta_tokens": nrm(ks[1], (N_META, D), jnp.float32),
        "ln_gain": 1.0 + 0.02 * nrm(ks[2], (DEPTH, 3, D), jnp.float32),
        "ln_bias": 0.02 * nrm(ks[3], (DEPTH, 3, D), jnp.float32),
        "ffn_w_in": nrm(ks[4], (DEPTH, 2, D, 2 * F), jnp.float32) * D ** -0.5,
        "ffn_w_out": nrm(ks[5], (DEPTH, 2, F, D), jnp.float32) * (F ** -0.5 * DEEPNORM_BETA),
        "conv_w_in": nrm(ks[6], (N_CONV_LAYERS, D, 3 * D), jnp.float32) * D ** -0.5,
        "conv_w": nrm(ks[7], (N_CONV_LAYERS, CONV_WIDTH, D), jnp.float32) * CONV_WIDTH ** -0.5,
        "conv_w_out": nrm(ks[8], (N_CONV_LAYERS, D, D), jnp.float32) * (D ** -0.5 * DEEPNORM_BETA),
        "gla_w_in": nrm(ks[9], (N_GLA_LAYERS, D, gla_in_width), jnp.float32) * D ** -0.5,
        "gla_w_gate_up": nrm(ks[10], (N_GLA_LAYERS, GLA_GATE_RANK, GLA_DK), jnp.float32) * GLA_GATE_RANK ** -0.5,
        "gla_b_gate": 0.01 * nrm(ks[11], (N_GLA_LAYERS, GLA_DK), jnp.float32),
        "gla_norm_w": 1.0 + 0.02 * nrm(ks[12], (N_GLA_LAYERS, GLA_HEAD_V), jnp.float32),
        "gla_w_out": nrm(ks[13], (N_GLA_LAYERS, GLA_DV, D), jnp.float32) * (GLA_DV ** -0.5 * DEEPNORM_BETA),
    }

def reference(x, meta_tokens, ln_gain, ln_bias, ffn_w_in, ffn_w_out, conv_w_in, conv_w, conv_w_out,
              gla_w_in, gla_w_gate_up, gla_b_gate, gla_norm_w, gla_w_out):
    bsz = x.shape[0]
    meta = jnp.broadcast_to(meta_tokens[None].astype(x.dtype), (bsz, N_META, D_MODEL))
    h = jnp.concatenate([meta, x], axis=1)
    for i in range(DEPTH):
        h = layer_norm(DEEPNORM_ALPHA * h + 0.5 * swiglu_ffn(h, ffn_w_in[i, 0], ffn_w_out[i, 0]),
                       ln_gain[i, 0], ln_bias[i, 0])
        j = i // N_MIXERS
        if i % N_MIXERS == 0:
            mix = short_conv_mixer(h, conv_w_in[j], conv_w[j], conv_w_out[j])
        else:
            mix = gla_mixer(h, gla_w_in[j], gla_w_gate_up[j], gla_b_gate[j], gla_norm_w[j], gla_w_out[j])
        h = layer_norm(DEEPNORM_ALPHA * h + mix, ln_gain[i, 1], ln_bias[i, 1])
        h = layer_norm(DEEPNORM_ALPHA * h + 0.5 * swiglu_ffn(h, ffn_w_in[i, 1], ffn_w_out[i, 1]),
                       ln_gain[i, 2], ln_bias[i, 2])
    return h[:, N_META:]


_drawn_inputs = setup_inputs


def setup_inputs(seed=0):
    import zlib

    import numpy as np

    out = dict(_drawn_inputs(seed))
    spreads = {}
    factors = {'gla_b_gate': 8.0, 'gla_norm_w': 8.0}
    for name, (base, spread) in spreads.items():
        noise = np.random.default_rng([zlib.crc32(name.encode()), seed]).standard_normal(out[name].shape)
        drawn = base * np.exp(spread * noise) if base else spread * noise
        out[name] = __import__('jax').numpy.asarray(drawn.astype(out[name].dtype))
    for name, factor in factors.items():
        out[name] = (out[name] * factor).astype(out[name].dtype)
    return out
```

```python
from contextlib import ExitStack

import concourse.bass as bass
from concourse import mybir

F32 = mybir.dt.float32
F32R = mybir.dt.float32r
ALU = mybir.AluOpType
ACT = mybir.ActivationFunctionType

P = 128
LN_EPS = 1e-5
RMS_EPS = 1e-6
RING = 6
KU = 8


def hybrid_trunk(nc, x, meta_tokens, ln_gain, ln_bias, ffn_w_in, ffn_w_out, conv_w_in, conv_w,
                 conv_w_out, gla_w_in, gla_w_gate_up, gla_b_gate, gla_norm_w, gla_w_out, out):
    _, SEQ, D = x.shape
    META = meta_tokens.shape[0]
    DEPTH = ln_gain.shape[0]
    F = ffn_w_out.shape[2]
    TAPS = conv_w.shape[1]
    RANK, DK = gla_w_gate_up.shape[1:]
    T = META + SEQ
    KD = D // P
    KF = F // P
    HEADS = DK // P
    VT = KD // HEADS
    HV = VT * P
    CH = 64
    NC = SEQ // CH
    KT0 = META + (NC - 1) * CH
    ALPHA = (2.0 * DEPTH) ** 0.25
    SETS = 3
    assert D == KU * P and META < CH // 2 and gla_norm_w.shape[1] == HV and DEPTH == 2

    FFN_IN, FFN_OUT = 2 * KF, 3 * KD
    K_PARTS = [(0, 8), (8, 16), (16, KF)]
    GLA_TILES = 1 + KD // 2 + KD // 2 + KD + KD
    unit0, at = {}, 0
    for name, count in [("f0", FFN_IN + FFN_OUT), ("conv", 4 * KD), ("f1", FFN_IN + FFN_OUT),
                        ("f2", FFN_IN + FFN_OUT), ("gla", GLA_TILES + KD), ("f3", FFN_IN + FFN_OUT)]:
        unit0[name] = at
        at += count
    UNITS = at
    FFN_NORM = [0, 2, 3, 5]
    CONV_NORM, GLA_NORM = 1, 4
    LAST_NORM = 3 * DEPTH - 1

    ctx = ExitStack()
    with ctx:
        def sb(name, shape, dt=F32):
            return ctx.enter_context(nc.sbuf_tensor(name, shape, dt))

        def sem(name):
            return ctx.enter_context(nc.semaphore(name))

        raw = sb("raw_weights", [P, RING, KU * P])
        w_hi = sb("weights_hi", [P, RING, KU * P], F32R)
        w_lo = sb("weights_lo", [P, RING, KU * P], F32R)
        x_hi = sb("x_hi", [P, KD, T], F32R)
        x_lo = sb("x_lo", [P, KD, T], F32R)
        resid = sb("resid", [P, KD, T])
        consts = sb("consts", [P, 6 * KD * 2 + TAPS * KD + VT])
        ident = sb("ident", [P, P])
        mean128 = sb("mean128", [P, P])
        meanD = sb("meanD", [P, P])
        meanV = sb("meanV", [P, P])
        eps = sb("eps", [P, 2])
        shift = sb("shift", [P, T])
        total = sb("total", [P, T])
        total_sq = sb("total_sq", [P, T])
        sq = sb("sq", [P, 2, T])
        mean = sb("mean", [P, T])
        mean_sq = sb("mean_sq", [P, T])
        var = sb("var", [P, T])
        std = sb("std", [P, T])
        rstd = sb("rstd", [P, T])
        scaled = sb("scaled", [P, 3, T])
        h_f = sb("h_f", [P, 3, T])
        silu_g = sb("silu_g", [P, SETS, T])
        prod = sb("prod", [P, SETS, T])

        with ExitStack() as inner:
            mid_hi = inner.enter_context(nc.sbuf_tensor("mid_hi", [P, KF, T], F32R))
            mid_lo = inner.enter_context(nc.sbuf_tensor("mid_lo", [P, KF, T], F32R))
        with ExitStack() as first:
            x_tok = first.enter_context(nc.sbuf_tensor("x_tok", [P, SEQ // P, D], F32))
            meta_tok = first.enter_context(nc.sbuf_tensor("meta_tok", [META, D], F32))
            const_rows = first.enter_context(nc.sbuf_tensor("const_rows", [P, P], F32))
        with ExitStack() as final:
            out_tok = final.enter_context(nc.sbuf_tensor("out_tok", [P, SEQ // P, D], F32))
        with ExitStack() as conv:
            cu = conv.enter_context(nc.sbuf_tensor("cu", [P, 2, TAPS - 1 + T], F32))
            u_sb = conv.enter_context(nc.sbuf_tensor("u_sb", [P, 2, T], F32))
            conv_t = conv.enter_context(nc.sbuf_tensor("conv_t", [P, 2, T], F32))
            yc_hi = conv.enter_context(nc.sbuf_tensor("yc_hi", [P, KD, T], F32R))
            yc_lo = conv.enter_context(nc.sbuf_tensor("yc_lo", [P, KD, T], F32R))
        gla = ctx.enter_context(ExitStack())

        def gb(name, shape, dt=F32):
            return gla.enter_context(nc.sbuf_tensor(name, shape, dt))

        y_hi = gb("y_hi", [P, KD, SEQ], F32R)
        y_lo = gb("y_lo", [P, KD, SEQ], F32R)
        kT = gb("kT", [P, HEADS, T])
        qT = gb("qT", [P, HEADS, SEQ])
        q_pos = gb("q_pos", [P, HEADS, SEQ])
        k_st = gb("k_st", [P, 2, KT0])
        gate_area = gb("gate_area", [P, 2, (NC + 1) * DK])
        log_a = gate_area[0:CH, 0, :].rearrange("p (c n) -> p c n", c=NC + 1)
        soft = gate_area[0:CH, 1, :].rearrange("p (c n) -> p c n", c=NC + 1)
        o_sb = gate_area[:, 0, 0:KD * SEQ].rearrange("p (m t) -> p m t", m=KD)
        silu_out = gate_area[:, 1, 0:KD * SEQ].rearrange("p (m t) -> p m t", m=KD)
        b_sb = h_f[:, 0:2, :]
        d_ref = scaled[:, 0:2, 0:SEQ]
        d_last = gb("d_last", [P, 2, KT0])
        e_buf = silu_g[:, :, 0:SEQ]
        e_last = gb("e_last", [P, KT0])
        decay = gb("decay", [P, HEADS, NC])
        vT = prod[:, 0:2, :]
        v_tok = gb("v_tok", [CH, 2, NC + 1, HV])
        k_tok = gb("k_tok", [CH, 2, NC, P])
        sT = gb("sT", [CH, 2, SEQ])
        state = gb("state", [P, NC, HV])
        o_sq = gb("o_sq", [P, VT, SEQ])
        ms_halves = gate_area[:, :, KD * SEQ:KD * SEQ + HEADS * SEQ // 2]

        def ms(h):
            return ms_halves[:, h // 2, (h % 2) * SEQ:(h % 2 + 1) * SEQ]

        y_t = q_pos[:, 0:2, :]
        gzT = sb("gzT", [RANK + 1, T])
        gate_up = sb("gate_up", [RANK + 1, DK])
        cum = sb("cum", [CH, CH])

        bank = [ctx.enter_context(nc.psum_tensor(f"bank{i}", [P, 512], F32)) for i in range(8)]

        raw_landed = [sem(f"raw_landed{i}") for i in range(RING)]
        hi_split, lo_split, unit_used = sem("hi_split"), sem("lo_split"), sem("unit_used")
        rows_landed, x_landed, gate_landed = sem("rows_landed"), sem("x_landed"), sem("gate_landed")
        ident_zeroed, masks_set, fills_done = sem("ident_zeroed"), sem("masks_set"), sem("fills_done")
        consts_turned, consts_ready = sem("consts_turned"), sem("consts_ready")
        x_turned, h0_ready = sem("x_turned"), sem("h0_ready")
        xhi_ready, xlo_ready, resid_ready = sem("xhi_ready"), sem("xlo_ready"), sem("resid_ready")
        silu_ready, prod_ready = sem("silu_ready"), sem("prod_ready")
        midhi_ready, mid_ready = sem("midhi_ready"), sem("mid_ready")
        z_ready, shift_meaned, shift_copied = sem("z_ready"), sem("shift_meaned"), sem("shift_copied")
        shifted, sq_ready, total_ready, totals_ready = sem("shifted"), sem("sq_ready"), sem("total_ready"), sem("totals_ready")
        stat_ready, mean_copied, meansq_ready = sem("stat_ready"), sem("mean_copied"), sem("meansq_ready")
        centred, var_ready, std_ready, rstd_ready = sem("centred"), sem("var_ready"), sem("std_ready"), sem("rstd_ready")
        scaled_ready, h_ready = sem("scaled_ready"), sem("h_ready")
        pad_zeroed, u_copied, conv_step, yc_ready = sem("pad_zeroed"), sem("u_copied"), sem("conv_step"), sem("yc_ready")
        gz_ones, gla_evac = sem("gz_ones"), sem("gla_evac")
        logits_made, logits_copied, soft_step, log_a_ready = sem("logits_made"), sem("logits_copied"), sem("soft_step"), sem("log_a_ready")
        cum_made, b_copied, diffs_ready = sem("cum_made"), sem("b_copied"), sem("diffs_ready")
        exps_ready, kst_ready, decayed = sem("exps_ready"), sem("kst_ready"), sem("decayed")
        v_turned, v_tok_ready = sem("v_turned"), sem("v_tok_ready")
        k_turned, k_tok_ready = sem("k_turned"), sem("k_tok_ready")
        scores_made, scores_copied, scores_masked = sem("scores_made"), sem("scores_copied"), sem("scores_masked")
        outer_made, state_ready = sem("outer_made"), sem("state_ready")
        o_made, o_copied, o_squared = sem("o_made"), sem("o_copied"), sem("o_squared")
        ms_made, ms_copied, rms_root, rms_ready = sem("ms_made"), sem("ms_copied"), sem("rms_root"), sem("rms_ready")
        y_step, y_ready = sem("y_step"), sem("y_ready")
        out_turned, out_copied, out_stored = sem("out_turned"), sem("out_copied"), sem("out_stored")

        def ln_gain_col(q, k):
            return consts[:, q * KD + k:q * KD + k + 1]

        def ln_bias_col(q, k):
            return consts[:, (6 + q) * KD + k:(6 + q) * KD + k + 1]

        def conv_col(tap, m):
            return consts[:, bass.ds((12 + tap) * KD + m, 1)]

        def norm_col(vt):
            return consts[:, (12 + TAPS) * KD + vt:(12 + TAPS) * KD + vt + 1]

        def tokens(n):
            return slice(T - n, T)

        def span(c):
            return slice(0, META) if c == 0 else slice(META + (c - 1) * CH, META + c * CH)

        def rows(c):
            return META if c == 0 else CH

        def body(c):
            return slice((c - 1) * CH, c * CH)

        block = ctx.enter_context(nc.Block())

        @block.sync
        def _(sp):
            def load(n, source, step=0):
                if n >= RING:
                    sp.wait_ge(lo_split, n + 1 - RING + step * RING)
                cols = source.shape[-1]
                dst = raw[:, n % RING, :].rearrange("p (k c) -> p k c", c=P)[:, 0:source.shape[1], 0:cols]
                sp.dma_start(dst, source).then_inc(raw_landed[n % RING], 16)

            def columns(w):
                return w.rearrange("(k p) n -> p k n", p=P)

            def load_ffn(f, n0):
                w_in = columns(ffn_w_in[f // 2, f % 2])
                w_out = columns(ffn_w_out[f // 2, f % 2])

                def tile_pair(n, t, step=0):
                    load(n, w_in[:, :, bass.ds(t * P, P)], step)
                    load(n + 1, w_in[:, :, bass.ds(F + t * P, P)], step)

                for t in range(4):
                    tile_pair(n0 + 2 * t, t)
                with sp.Fori(0, (KF - 4) // SETS) as i:
                    for j in range(SETS):
                        tile_pair(n0 + 8 + 2 * j, i * SETS + (4 + j), i)
                with sp.Fori(0, KD // 2) as i:
                    for j in range(2):
                        for u, (k0, k1) in enumerate(K_PARTS):
                            load(n0 + FFN_IN + 3 * j + u, w_out[:, k0:k1, bass.ds(i * 2 * P + j * P, P)], i)

            sp.dma_start(x_tok[:], x[0].rearrange("(b p) d -> p b d", p=P)).then_inc(x_landed, 16)
            sp.dma_start(meta_tok[:], meta_tokens).then_inc(x_landed, 16)
            load_ffn(0, unit0["f0"])
            n = unit0["conv"]
            w = columns(conv_w_in[0])
            with sp.Fori(0, KD // 2) as i:
                for j in range(2):
                    for part in range(3):
                        load(n + 3 * j + part, w[:, :, bass.ds(part * D + j * P + i * 2 * P, P)], i)
            w = columns(conv_w_out[0])
            for m in range(KD):
                load(n + 3 * KD + m, w[:, :, m * P:(m + 1) * P])
            load_ffn(1, unit0["f1"])
            load_ffn(2, unit0["f2"])
            n = unit0["gla"]
            w = columns(gla_w_in[0])
            load(n, w[:, :, 2 * DK + 2 * D:2 * DK + 2 * D + RANK])
            for m in range(GLA_TILES - 1):
                c0 = DK + m * P if m < HEADS else (m - HEADS) * P if m < 2 * HEADS else m * P
                load(n + 1 + m, w[:, :, c0:c0 + P])
            w = columns(gla_w_out[0])
            for m in range(KD):
                load(n + GLA_TILES + m, w[:, :, m * P:(m + 1) * P])
            load_ffn(3, unit0["f3"])
            halves = 2
            for part in range(halves):
                sp.wait_ge(out_copied, (part + 1) * (SEQ // P))
                cols = slice(part * D // halves, (part + 1) * D // halves)
                sp.dma_start(out[0].rearrange("(b p) d -> p b d", p=P)[:, :, cols],
                             out_tok[:, :, cols]).then_inc(out_stored, 16)
            sp.wait_ge(out_stored, 16 * halves)

        @block.gpsimd
        def _(pool):
            row = 0
            for source in (ln_gain.rearrange("l s (k p) -> (l s k) p", p=P),
                           ln_bias.rearrange("l s (k p) -> (l s k) p", p=P),
                           conv_w.rearrange("l s (k p) -> (l s k) p", p=P),
                           gla_norm_w.rearrange("l (k p) -> (l k) p", p=P)):
                pool.dma_start(const_rows[row:row + source.shape[0], :], source).then_inc(rows_landed, 16)
                row += source.shape[0]
            pool.dma_start(gate_up[0:RANK, :], gla_w_gate_up[0]).then_inc(gate_landed, 16)
            pool.dma_start(gate_up[RANK:RANK + 1, :], gla_b_gate).then_inc(gate_landed, 16)
            nc.gpsimd.memset(ident[:], 0.0).then_inc(ident_zeroed, 1)
            nc.gpsimd.memset(cum[:], 1.0 / 16.0).then_inc(ident_zeroed, 1)
            pool.wait_ge(ident_zeroed, 2)
            nc.gpsimd.affine_select(out=ident[:], in_=ident[:], compare_op=ALU.not_equal, fill=1.0, base=0,
                                    pattern=[[-1, P]], channel_multiplier=1).then_inc(masks_set, 1)
            nc.gpsimd.affine_select(out=cum[:], in_=cum[:], compare_op=ALU.is_ge, fill=0.0, base=0,
                                    pattern=[[1, CH]], channel_multiplier=-1).then_inc(masks_set, 1)
            for h in range(HEADS):
                pool.wait_ge(scores_copied, h + 1)
                s = sT[:, h % 2, :].rearrange("p (c i) -> p c i", i=CH)
                nc.gpsimd.affine_select(out=s, in_=s, compare_op=ALU.is_ge, fill=0.0, base=0,
                                        pattern=[[0, NC], [1, CH]], channel_multiplier=-1).then_inc(scores_masked, 1)

        @block.scalar
        def _(act):
            def split_hi(n, step=0):
                if n >= RING:
                    act.wait_ge(unit_used, n + 1 - RING + step * RING)
                act.wait_ge(raw_landed[n % RING], (step + (n // RING + 1)) * 16)
                nc.scalar.activation(w_hi[:, n % RING, :], raw[:, n % RING, :], ACT.Copy).then_inc(hi_split, 1)

            def square_chunk(q, mo, n_tok, step=0):
                cols = tokens(n_tok)
                if mo == 0:
                    act.wait_ge(shifted, q + 1)
                    nc.scalar.activation(total_sq[:, cols], resid[:, 0, cols], ACT.Square).then_inc(sq_ready, 1)
                    return
                c = KD * q + mo
                act.wait_ge(z_ready, step * 2 + (c + 1))
                if mo >= 2:
                    act.wait_ge(totals_ready, step * 2 + ((KD - 2) * q + mo - 1))
                elif q:
                    act.wait_ge(stat_ready, 2 * q)
                nc.scalar.activation(sq[:, mo % 2, cols], resid[:, bass.ds(step * 2 + mo, 1), cols],
                                     ACT.Square).then_inc(sq_ready, 1)

            def normalise(q, n_tok):
                cols = tokens(n_tok)
                act.wait_ge(var_ready, q + 1)
                nc.scalar.activation(std[:, cols], var[:, cols], ACT.Sqrt, bias=eps[:, 0:1]).then_inc(std_ready, 1)
                for k in range(KD):
                    act.wait_ge(scaled_ready, KD * q + k + 1)
                    if q == LAST_NORM:
                        nc.scalar.activation(resid[:, k, cols], scaled[:, k % 3, cols], ACT.Identity,
                                             bias=ln_bias_col(q, k)).then_inc(h_ready, 1)
                        if k % (KD // 2) == KD // 2 - 1:
                            copy_out(k // (KD // 2))
                        continue
                    nc.scalar.activation(x_hi[:, k, cols], scaled[:, k % 3, cols], ACT.Identity,
                                         bias=ln_bias_col(q, k)).then_inc(xhi_ready, 1)
                    if k >= 3:
                        act.wait_ge(xlo_ready, KD * (q + 1) + k - 2)
                    nc.scalar.activation(h_f[:, k % 3, cols], scaled[:, k % 3, cols], ACT.Identity,
                                         bias=ln_bias_col(q, k)).then_inc(h_ready, 1)
                    act.wait_ge(h_ready, KD * q + k + 1)
                    nc.scalar.mul(resid[:, k, cols], h_f[:, k % 3, cols], ALPHA).then_inc(resid_ready, 1)

            def copy_out(part):
                act.wait_ge(out_turned, part + 1)
                for b in range(SEQ // P):
                    nc.scalar.activation(out_tok[:, b, part * D // 2:(part + 1) * D // 2], bank[2 * part + b][:],
                                         ACT.Copy).then_inc(out_copied, 1)

            def out_projection(q, n0, parts, n_tok):
                def chunk(mo, step=0):
                    n = n0 + parts * mo
                    for u in range(parts - 1):
                        if n + u + RING < UNITS:
                            split_hi(n + u + RING, step)
                    if mo == 1:
                        square_chunk(q, 0, n_tok)
                    if mo >= 1:
                        square_chunk(q, mo, n_tok, step)
                    if mo == KD - 1:
                        normalise(q, n_tok)
                    if n + parts - 1 + RING < UNITS:
                        split_hi(n + parts - 1 + RING, step)
                if parts == 3:
                    chunk(0)
                    chunk(1)
                    with act.Fori(0, (KD - 4) // 2) as i:
                        chunk(2, i)
                        chunk(3, i)
                    chunk(KD - 2)
                    chunk(KD - 1)
                else:
                    for mo in range(KD):
                        chunk(mo)

            def ffn(f, n0, n_tok):
                cols = tokens(n_tok)

                def silu(t, step=0):
                    g = KF * f + t
                    act.wait_ge(unit_used, step * RING + (n0 + 2 * t + 1))
                    if g >= SETS:
                        act.wait_ge(mid_ready, step * SETS + (g - SETS + 1))
                    nc.scalar.activation(silu_g[:, t % SETS, cols], bank[2 * (t % SETS)][:, 0:n_tok],
                                         ACT.Silu).then_inc(silu_ready, 1)

                def tile(t, step=0):
                    n = n0 + 2 * t
                    split_hi(n + RING, step)
                    silu(t, step)
                    split_hi(n + 1 + RING, step)

                silu(0)
                split_hi(n0 + RING)
                silu(1)
                for u in range(1, 4):
                    split_hi(n0 + u + RING)
                for t in range(2, 2 + SETS):
                    tile(t)
                with act.Fori(0, (KF - 4) // SETS - 1) as i:
                    for t in range(2 + SETS, 2 + 2 * SETS):
                        tile(t, i)
                tile(KF - 2)
                tile(KF - 1)
                out_projection(FFN_NORM[f], n0 + FFN_IN, 3, n_tok)

            act.wait_ge(consts_turned, 1)
            nc.scalar.activation(consts[:], bank[5][:, 0:consts.shape[1]], ACT.Copy).then_inc(consts_ready, 1)
            for k in range(KD):
                act.wait_ge(x_turned, k + 1)
                if k >= 3:
                    act.wait_ge(xlo_ready, k - 2)
                nc.scalar.activation(h_f[:, k % 3, :], bank[6 + k % 2][:, 0:T], ACT.Copy).then_inc(h0_ready, 1)
                act.wait_ge(h0_ready, k + 1)
                nc.scalar.activation(x_hi[:, k, :], h_f[:, k % 3, :], ACT.Copy).then_inc(xhi_ready, 1)
                nc.scalar.mul(resid[:, k, :], h_f[:, k % 3, :], ALPHA).then_inc(resid_ready, 1)
            for n in range(RING):
                split_hi(n)
            act.wait_ge(consts_ready, 1)
            act.wait_ge(fills_done, 1)

            ffn(0, unit0["f0"], T)

            n0 = unit0["conv"]

            def copy_u(m, step=0):
                act.wait_ge(unit_used, step * RING + (n0 + 3 * m + 3))
                if m >= 2:
                    act.wait_ge(yc_ready, step * 2 + (m - 1))
                nc.scalar.activation(u_sb[:, m % 2, :], bank[3 * (m % 2) + 2][:, 0:T], ACT.Copy).then_inc(u_copied, 1)

            def conv_chunk(m, step=0):
                n = n0 + 3 * m
                split_hi(n + RING, step)
                split_hi(n + 1 + RING, step)
                copy_u(m, step)
                split_hi(n + 2 + RING, step)

            conv_chunk(0)
            conv_chunk(1)
            with act.Fori(0, KD // 2 - 1) as i:
                conv_chunk(2, i)
                conv_chunk(3, i)
            out_projection(CONV_NORM, n0 + 3 * KD, 1, T)

            ffn(1, unit0["f1"], T)
            ffn(2, unit0["f2"], T)

            n0 = unit0["gla"]
            act.wait_ge(gz_ones, 1)

            def gla_tile(j):
                act.wait_ge(unit_used, n0 + j + 1)
                ps = bank[j if j < 4 else j % 2]
                if j == 0:
                    nc.scalar.activation(gzT[0:RANK, :], ps[0:RANK, 0:T], ACT.Copy).then_inc(gla_evac, 1)
                elif j <= HEADS:
                    nc.scalar.activation(kT[:, j - 1, :], ps[:, 0:T], ACT.Copy).then_inc(gla_evac, 1)
                elif j <= 2 * HEADS:
                    nc.scalar.mul(qT[:, j - 1 - HEADS, :], ps[:, 0:SEQ], float(P) ** -0.5).then_inc(gla_evac, 1)
                elif j <= 2 * HEADS + KD:
                    v = j - 1 - 2 * HEADS
                    if v >= 2:
                        act.wait_ge(v_turned, v - 1)
                    nc.scalar.activation(vT[:, v % 2, :], ps[:, 0:T], ACT.Copy).then_inc(gla_evac, 1)
                else:
                    m = j - 1 - 2 * HEADS - KD
                    if m == 0:
                        act.wait_ge(log_a_ready, 2)
                    nc.scalar.activation(silu_out[:, m, :], ps[:, 0:SEQ], ACT.Silu).then_inc(gla_evac, 1)
                split_hi(n0 + j + RING)

            def softplus():
                act.wait_ge(logits_copied, NC + 1)
                areas = [(soft[0:META, 0, :], log_a[0:META, 0, :]), (soft[:, 1:, :], log_a[:, 1:, :])]
                for s, a in areas:
                    nc.scalar.activation(s, a, ACT.Abs).then_inc(soft_step, 1)
                act.wait_ge(soft_step, 2)
                for s, a in areas:
                    nc.scalar.activation(s, s, ACT.Exp, scale=-1.0).then_inc(soft_step, 1)
                act.wait_ge(soft_step, 4)
                for s, a in areas:
                    nc.scalar.activation(s, s, ACT.Ln, bias=1.0).then_inc(soft_step, 1)

            def decays(h):
                act.wait_ge(diffs_ready, 2 * h + 2)
                if h >= 1:
                    act.wait_ge(decayed, 2 * h)
                nc.scalar.activation(e_last[:], d_last[:, h % 2, :], ACT.Exp, scale=-1.0).then_inc(exps_ready, 1)
                nc.scalar.activation(e_buf[:, 0, :], d_ref[:, h % 2, :], ACT.Exp).then_inc(exps_ready, 1)
                nc.scalar.activation(e_buf[:, 1, :], d_ref[:, h % 2, :], ACT.Exp, scale=-1.0).then_inc(exps_ready, 1)
                nc.scalar.activation(e_buf[:, 2, :], b_sb[:, h % 2, META:T], ACT.Exp).then_inc(exps_ready, 1)
                nc.scalar.activation(decay[:, h, :], b_sb[:, h % 2, META - 1:KT0:CH], ACT.Exp).then_inc(exps_ready, 1)

            def copy_o(h):
                act.wait_ge(o_made, h + 1)
                o = o_sb[:, VT * h:VT * h + VT, :]
                nc.scalar.activation(o, bank[3][:].rearrange("p (v t) -> p v t", v=VT), ACT.Copy).then_inc(o_copied, 1)
                act.wait_ge(o_copied, h + 1)
                if h >= 1:
                    act.wait_ge(ms_made, h)
                nc.scalar.activation(o_sq[:], o, ACT.Square).then_inc(o_squared, 1)

            for j in range(GLA_TILES):
                gla_tile(j)
                if j == 5:
                    softplus()
                if 9 <= j < 9 + HEADS:
                    decays(j - 9)
                if j >= 13 and (j - 13) % 2 == 0 and (j - 13) // 2 < HEADS:
                    copy_o((j - 13) // 2)
                if j == 20:
                    act.wait_ge(ms_copied, HEADS)
                    nc.scalar.activation(ms_halves, ms_halves, ACT.Sqrt, bias=eps[:, 1:2]).then_inc(rms_root, 1)
            out_projection(GLA_NORM, n0 + GLA_TILES, 1, SEQ)

            ffn(3, unit0["f3"], SEQ)

        @block.vector
        def _(dve):
            def split_lo(n, step=0):
                dve.wait_ge(hi_split, step * RING + (n + 1))
                s = n % RING
                nc.vector.tensor_tensor(w_lo[:, s, :], raw[:, s, :], w_hi[:, s, :].bitcast(F32),
                                        ALU.subtract).then_inc(lo_split, 1)

            def z_chunk(q, mo, n_tok, step=0):
                cols = tokens(n_tok)
                scale = 0.5 if q in FFN_NORM else 1.0
                c = KD * q + mo
                z = resid[:, bass.ds(step * 2 + mo, 1), cols]
                ps = bank[6 + mo % 2][:, 0:n_tok]
                if mo == 0:
                    dve.wait_ge(resid_ready, KD * (q + 1))
                if mo == 1:
                    dve.wait_ge(shift_meaned, q + 1)
                    nc.vector.tensor_copy(shift[:, cols], bank[4][:, 0:n_tok]).then_inc(shift_copied, 1)
                    dve.wait_ge(shift_copied, q + 1)
                    everything = resid[:, :, cols]
                    nc.vector.tensor_tensor(everything, everything,
                                            shift[:, cols].unsqueeze(1).broadcast_to([P, KD, n_tok]),
                                            ALU.subtract).then_inc(shifted, 1)
                    dve.wait_ge(shifted, q + 1)
                nc.vector.scalar_tensor_tensor(out=z, in0=ps, scalar=scale, in1=z, op0=ALU.mult,
                                               op1=ALU.add).then_inc(z_ready, 1)
                if 1 <= mo < KD - 1:
                    dve.wait_ge(z_ready, step * 2 + (c + 1))
                    before = resid[:, 0:1, cols] if mo == 1 else total[:, cols]
                    nc.vector.tensor_tensor(total[:, cols], before, z, ALU.add).then_inc(total_ready, 1)
                    dve.wait_ge(sq_ready, step * 2 + (c + 1))
                    nc.vector.tensor_tensor(total_sq[:, cols], total_sq[:, cols], sq[:, mo % 2, cols],
                                            ALU.add).then_inc(totals_ready, 1)

            def normalise(q, n_tok):
                cols = tokens(n_tok)

                def centre(k):
                    nc.vector.tensor_tensor(resid[:, k, cols], resid[:, k, cols], mean[:, cols],
                                            ALU.subtract).then_inc(centred, 1)

                def x_low(k):
                    dve.wait_ge(h_ready, KD * q + k + 1)
                    nc.vector.tensor_tensor(x_lo[:, k, cols], h_f[:, k % 3, cols], x_hi[:, k, cols].bitcast(F32),
                                            ALU.subtract).then_inc(xlo_ready, 1)

                dve.wait_ge(stat_ready, 2 * q + 1)
                nc.vector.tensor_copy(mean[:, cols], bank[4][:, 0:n_tok]).then_inc(mean_copied, 1)
                dve.wait_ge(mean_copied, q + 1)
                nc.vector.tensor_tensor(mean_sq[:, cols], mean[:, cols], mean[:, cols], ALU.mult).then_inc(meansq_ready, 1)
                centre(0)
                dve.wait_ge(stat_ready, 2 * q + 2)
                dve.wait_ge(meansq_ready, q + 1)
                nc.vector.tensor_tensor(var[:, cols], bank[5][:, 0:n_tok], mean_sq[:, cols], ALU.subtract).then_inc(var_ready, 1)
                centre(1)
                dve.wait_ge(std_ready, q + 1)
                nc.vector.reciprocal(rstd[:, cols], std[:, cols]).then_inc(rstd_ready, 1)
                dve.wait_ge(rstd_ready, q + 1)
                for k in range(KD):
                    dve.wait_ge(centred, KD * q + k + 1)
                    if k >= 3:
                        dve.wait_ge(h_ready, KD * q + k - 2)
                    nc.vector.scalar_tensor_tensor(out=scaled[:, k % 3, cols], in0=resid[:, k, cols],
                                                   scalar=ln_gain_col(q, k), in1=rstd[:, cols], op0=ALU.mult,
                                                   op1=ALU.mult).then_inc(scaled_ready, 1)
                    if k + 2 < KD:
                        centre(k + 2)
                    if k >= 1 and q != LAST_NORM:
                        x_low(k - 1)
                if q != LAST_NORM:
                    x_low(KD - 1)

            def out_projection(q, n0, parts, n_tok):
                def chunk(mo, step=0):
                    n = n0 + parts * mo
                    for u in range(parts - 1):
                        if n + u + RING < UNITS:
                            split_lo(n + u + RING, step)
                    dve.wait_ge(unit_used, step * RING + (n + parts))
                    z_chunk(q, mo, n_tok, step)
                    if mo == KD - 1:
                        normalise(q, n_tok)
                    if n + parts - 1 + RING < UNITS:
                        split_lo(n + parts - 1 + RING, step)
                if parts == 3:
                    chunk(0)
                    chunk(1)
                    with dve.Fori(0, (KD - 4) // 2) as i:
                        chunk(2, i)
                        chunk(3, i)
                    chunk(KD - 2)
                    chunk(KD - 1)
                else:
                    for mo in range(KD):
                        chunk(mo)

            def ffn(f, n0, n_tok):
                cols = tokens(n_tok)

                def gate_times_up(t, step=0):
                    g = KF * f + t
                    s = t % SETS
                    dve.wait_ge(silu_ready, step * SETS + (g + 1))
                    dve.wait_ge(unit_used, step * RING + (n0 + 2 * t + 2))
                    nc.vector.tensor_tensor(prod[:, s, cols], bank[2 * s + 1][:, 0:n_tok], silu_g[:, s, cols],
                                            ALU.mult).then_inc(prod_ready, 1)
                    dve.wait_ge(prod_ready, step * SETS + (g + 1))
                    at_t = bass.ds(step * SETS + t, 1)
                    nc.vector.tensor_copy(mid_hi[:, at_t, cols], prod[:, s:s + 1, cols]).then_inc(midhi_ready, 1)
                    dve.wait_ge(midhi_ready, step * SETS + (g + 1))
                    nc.vector.tensor_tensor(mid_lo[:, at_t, cols], prod[:, s:s + 1, cols],
                                            mid_hi[:, at_t, cols].bitcast(F32), ALU.subtract).then_inc(mid_ready, 1)

                def tile(t, step=0):
                    n = n0 + 2 * t
                    split_lo(n + RING, step)
                    gate_times_up(t, step)
                    split_lo(n + 1 + RING, step)

                gate_times_up(0)
                split_lo(n0 + RING)
                gate_times_up(1)
                for u in range(1, 4):
                    split_lo(n0 + u + RING)
                with dve.Fori(0, (KF - 4) // SETS) as i:
                    for t in range(2, 2 + SETS):
                        tile(t, i)
                tile(KF - 2)
                tile(KF - 1)
                out_projection(FFN_NORM[f], n0 + FFN_IN, 3, n_tok)

            nc.vector.memset(mean128[:], 1.0 / P)
            nc.vector.memset(meanD[:], 1.0 / D)
            nc.vector.memset(meanV[:], 1.0 / HV)
            nc.vector.memset(eps[:, 0:1], LN_EPS)
            nc.vector.memset(gzT[:], 1.0).then_inc(gz_ones, 1)
            nc.vector.memset(eps[:, 1:2], RMS_EPS).then_inc(fills_done, 1)
            for k in range(KD):
                dve.wait_ge(xhi_ready, k + 1)
                nc.vector.tensor_tensor(x_lo[:, k, :], h_f[:, k % 3, :], x_hi[:, k, :].bitcast(F32),
                                        ALU.subtract).then_inc(xlo_ready, 1)
            for n in range(RING):
                split_lo(n)
            dve.wait_ge(consts_ready, 1)

            ffn(0, unit0["f0"], T)

            n0 = unit0["conv"]
            nc.vector.memset(cu[:, :, 0:TAPS - 1], 0.0).then_inc(pad_zeroed, 1)
            dve.wait_ge(pad_zeroed, 1)

            def convolve(m, step=0):
                s = m % 2
                done = 6 * m
                dve.wait_ge(u_copied, step * 2 + (m + 1))
                b_ps, c_ps = bank[3 * s][:, 0:T], bank[3 * s + 1][:, 0:T]
                mm = step * 2 + m
                at_m = bass.ds(mm, 1)
                t0, t1 = conv_t[:, 0:1, :], conv_t[:, 1:2, :]
                nc.vector.tensor_tensor(cu[:, s, TAPS - 1:TAPS - 1 + T], c_ps, u_sb[:, s, :], ALU.mult).then_inc(conv_step, 1)
                dve.wait_ge(conv_step, step * 12 + (done + 1))
                nc.vector.tensor_scalar(t0, cu[:, s:s + 1, 0:T], conv_col(0, mm), None, ALU.mult).then_inc(conv_step, 1)
                dve.wait_ge(conv_step, step * 12 + (done + 2))
                nc.vector.scalar_tensor_tensor(out=t1, in0=cu[:, s:s + 1, 1:1 + T], scalar=conv_col(1, mm), in1=t0,
                                               op0=ALU.mult, op1=ALU.add).then_inc(conv_step, 1)
                dve.wait_ge(conv_step, step * 12 + (done + 3))
                nc.vector.scalar_tensor_tensor(out=t0, in0=cu[:, s:s + 1, 2:2 + T], scalar=conv_col(2, mm), in1=t1,
                                               op0=ALU.mult, op1=ALU.add).then_inc(conv_step, 1)
                dve.wait_ge(conv_step, step * 12 + (done + 4))
                nc.vector.tensor_tensor(t1, b_ps, t0, ALU.mult).then_inc(conv_step, 1)
                dve.wait_ge(conv_step, step * 12 + (done + 5))
                nc.vector.tensor_copy(yc_hi[:, at_m, :], t1).then_inc(conv_step, 1)
                dve.wait_ge(conv_step, step * 12 + (done + 6))
                nc.vector.tensor_tensor(yc_lo[:, at_m, :], t1, yc_hi[:, at_m, :].bitcast(F32),
                                        ALU.subtract).then_inc(yc_ready, 1)

            def conv_chunk(m, step=0):
                n = n0 + 3 * m
                split_lo(n + RING, step)
                split_lo(n + 1 + RING, step)
                convolve(m, step)
                split_lo(n + 2 + RING, step)

            conv_chunk(0)
            conv_chunk(1)
            with dve.Fori(0, KD // 2 - 1) as i:
                conv_chunk(2, i)
                conv_chunk(3, i)
            out_projection(CONV_NORM, n0 + 3 * KD, 1, T)

            ffn(1, unit0["f1"], T)
            ffn(2, unit0["f2"], T)

            n0 = unit0["gla"]

            def copy_logits():
                for c in range(NC + 1):
                    dve.wait_ge(logits_made, c + 1)
                    nc.vector.tensor_copy(log_a[0:rows(c), c, :], bank[4 + c % 2][0:rows(c), :]).then_inc(logits_copied, 1)

            def log_sigmoid():
                dve.wait_ge(soft_step, 6)
                for n, (a, s) in enumerate([(log_a[0:META, 0, :], soft[0:META, 0, :]),
                                            (log_a[:, 1:, :], soft[:, 1:, :])]):
                    nc.vector.scalar_tensor_tensor(out=a, in0=a, scalar=0.0, in1=s, op0=ALU.min,
                                                   op1=ALU.subtract).then_inc(log_a_ready, 1)

            def differences(h):
                s = h % 2
                dve.wait_ge(cum_made, h + 1)
                if h >= 2:
                    dve.wait_ge(exps_ready, 5 * (h - 1))
                nc.vector.tensor_copy(b_sb[:, s, :], bank[6 + s][:, 0:T]).then_inc(b_copied, 1)
                dve.wait_ge(b_copied, h + 1)
                b_main = b_sb[:, s, META:T].rearrange("p (c i) -> p c i", i=CH)
                b_ref = b_main[:, :, CH // 2:CH // 2 + 1].broadcast_to([P, NC, CH])
                nc.vector.tensor_tensor(d_ref[:, s, :].rearrange("p (c i) -> p c i", i=CH), b_main, b_ref,
                                        ALU.subtract)
                nc.vector.tensor_tensor(d_last[:, s, META:KT0].rearrange("p (c i) -> p c i", i=CH),
                                        b_main[:, 0:NC - 1, :], b_main[:, 0:NC - 1, CH - 1:CH].broadcast_to([P, NC - 1, CH]),
                                        ALU.subtract).then_inc(diffs_ready, 1)
                nc.vector.tensor_tensor(d_last[:, s, 0:META], b_sb[:, s, 0:META],
                                        b_sb[:, s, META - 1:META].broadcast_to([P, META]), ALU.subtract).then_inc(diffs_ready, 1)

            def apply_decays(h):
                dve.wait_ge(exps_ready, 5 * h + 1)
                dve.wait_ge(gla_evac, 1 + HEADS)
                if h >= 2:
                    dve.wait_ge(k_turned, h - 1)
                nc.vector.tensor_tensor(k_st[:, h % 2, :], kT[:, h, 0:KT0], e_last[:], ALU.mult).then_inc(kst_ready, 1)
                dve.wait_ge(exps_ready, 5 * h + 4)
                dve.wait_ge(gla_evac, 1 + 2 * HEADS)
                nc.vector.tensor_tensor(q_pos[:, h, :], qT[:, h, :], e_buf[:, 0, :], ALU.mult).then_inc(decayed, 1)
                dve.wait_ge(kst_ready, h + 1)
                nc.vector.tensor_tensor(kT[:, h, META:T], kT[:, h, META:T], e_buf[:, 1, :], ALU.mult)
                dve.wait_ge(decayed, 2 * h + 1)
                nc.vector.tensor_tensor(qT[:, h, :], qT[:, h, :], e_buf[:, 2, :], ALU.mult).then_inc(decayed, 1)

            def copy_v(v):
                h, vt = v // VT, v % VT
                dve.wait_ge(v_turned, v + 1)
                if h >= 2:
                    dve.wait_ge(o_made, h - 1)
                half = slice(vt * P, (vt + 1) * P)
                nc.vector.tensor_copy(v_tok[0:META, h % 2, 0, half], bank[2][0:META, 0:P])
                nc.vector.tensor_copy(v_tok[:, h % 2, 1:, half],
                                      bank[5][0:CH, :].rearrange("p (c n) -> p c n", n=P)).then_inc(v_tok_ready, 1)

            def copy_k(h):
                dve.wait_ge(k_turned, h + 1)
                nc.vector.tensor_copy(k_tok[0:META, h % 2, 0, :], bank[4][0:META, 0:P])
                nc.vector.tensor_copy(k_tok[:, h % 2, 1:, :],
                                      bank[4][0:CH, P:].rearrange("p (c n) -> p c n", n=P)).then_inc(k_tok_ready, 1)

            def copy_scores(h):
                dve.wait_ge(scores_made, h + 1)
                nc.vector.tensor_copy(sT[:, h % 2, :], bank[3][0:CH, 0:SEQ]).then_inc(scores_copied, 1)

            def states(h):
                dve.wait_ge(outer_made, h + 1)
                if h >= 1:
                    dve.wait_ge(o_made, h)
                dve.wait_ge(exps_ready, 5 * h + 5)
                for c in range(NC):
                    ps = bank[6 + c // 2][:, (c % 2) * HV:(c % 2 + 1) * HV]
                    if c == 0:
                        nc.vector.tensor_copy(state[:, 0, :], ps).then_inc(state_ready, 1)
                        continue
                    dve.wait_ge(state_ready, NC * h + c)
                    nc.vector.scalar_tensor_tensor(out=state[:, c, :], in0=state[:, c - 1, :],
                                                   scalar=decay[:, h, c:c + 1], in1=ps, op0=ALU.mult,
                                                   op1=ALU.add).then_inc(state_ready, 1)

            def copy_ms(h):
                dve.wait_ge(ms_made, h + 1)
                nc.vector.tensor_copy(ms(h), bank[4][:, 0:SEQ]).then_inc(ms_copied, 1)

            def rms():
                dve.wait_ge(rms_root, 1)
                nc.vector.reciprocal(ms_halves, ms_halves).then_inc(rms_ready, 1)

            def gate_output(m):
                s = m % 2
                dve.wait_ge(rms_ready, 1)
                nc.vector.scalar_tensor_tensor(out=y_t[:, 0, :], in0=o_sb[:, m, :], scalar=norm_col(m % VT),
                                               in1=ms(m // VT), op0=ALU.mult, op1=ALU.mult).then_inc(y_step, 1)
                dve.wait_ge(y_step, 3 * m + 1)
                dve.wait_ge(gla_evac, 2 + 2 * HEADS + KD + m)
                nc.vector.tensor_tensor(y_t[:, 1, :], y_t[:, 0, :], silu_out[:, m, :], ALU.mult).then_inc(y_step, 1)
                dve.wait_ge(y_step, 3 * m + 2)
                nc.vector.tensor_copy(y_hi[:, m, :], y_t[:, 1, :]).then_inc(y_step, 1)
                dve.wait_ge(y_step, 3 * m + 3)
                nc.vector.tensor_tensor(y_lo[:, m, :], y_t[:, 1, :], y_hi[:, m, :].bitcast(F32),
                                        ALU.subtract).then_inc(y_ready, 1)

            for j in range(GLA_TILES):
                split_lo(n0 + j + RING)
                if j == 4:
                    copy_logits()
                if j == 6:
                    log_sigmoid()
                if j == 8:
                    differences(0)
                    differences(1)
                if j == 9:
                    apply_decays(0)
                    differences(2)
                if j == 10:
                    apply_decays(1)
                    differences(3)
                if j == 11:
                    apply_decays(2)
                if 10 <= j < 10 + KD:
                    copy_v(j - 10)
                h, phase = (j - 11) // 2, (j - 11) % 2
                if j >= 11 and phase == 0 and h < HEADS:
                    copy_k(h)
                    if h == 1:
                        apply_decays(3)
                    copy_scores(h)
                if j >= 11 and phase == 1:
                    if h < HEADS:
                        states(h)
                    if 0 <= h - 1 < HEADS:
                        copy_ms(h - 1)
                if j == 21:
                    rms()
                if j >= 21:
                    gate_output(2 * (j - 21))
                    if j < 24:
                        gate_output(2 * (j - 21) + 1)
            gate_output(KD - 1)
            out_projection(GLA_NORM, n0 + GLA_TILES, 1, SEQ)

            ffn(3, unit0["f3"], SEQ)

        @block.tensor
        def _(pe):
            def block_of(w, n, k):
                return w[:, n % RING, k * P:(k + 1) * P]

            def multiply(ps, n, source, cols, k0=0, k1=KU, first=True, last=True, step=0, ready=None):
                hi, lo = source
                pe.wait_ge(lo_split, step * RING + (n + 1))
                for k in range(k0, k1):
                    if ready is not None:
                        pe.wait_ge(ready[0], ready[1] + k + 1)
                    w_h, w_l = block_of(w_hi, n, k - k0), block_of(w_lo, n, k - k0)
                    nc.tensor.matmul(ps, w_h, hi[:, k, cols], start=first and k == k0, stop=False)
                    nc.tensor.matmul(ps, w_h, lo[:, k, cols], start=False, stop=False)
                    mm = nc.tensor.matmul(ps, w_l, hi[:, k, cols], start=False, stop=last and k == k1 - 1)
                mm.then_inc(unit_used, 1)

            def multiply_together(outs, n0, gen):
                for u in range(len(outs)):
                    pe.wait_ge(lo_split, n0 + u + 1)
                for k in range(KD):
                    pe.wait_ge(xhi_ready, KD * gen + k + 1)
                    for u, (ps, cols) in enumerate(outs):
                        nc.tensor.matmul(ps, block_of(w_hi, n0 + u, k), x_hi[:, k, cols], start=k == 0, stop=False)
                        nc.tensor.matmul(ps, block_of(w_lo, n0 + u, k), x_hi[:, k, cols], start=False, stop=False)
                    pe.wait_ge(xlo_ready, KD * gen + k + 1)
                    for u, (ps, cols) in enumerate(outs):
                        mm = nc.tensor.matmul(ps, block_of(w_hi, n0 + u, k), x_lo[:, k, cols], start=False,
                                              stop=k == KD - 1)
                        if k == KD - 1:
                            mm.then_inc(unit_used, 1)

            def out_projection(q, n0, k_parts, source, ready, n_tok):
                src_cols = slice(0, n_tok) if source[0].shape[2] == n_tok else tokens(n_tok)
                cols = tokens(n_tok)
                parts = len(k_parts)

                def chunk(mo, step=0):
                    ps = bank[6 + mo % 2][:, 0:n_tok]
                    if mo >= 2:
                        pe.wait_ge(z_ready, step * 2 + (KD * q + mo - 1))
                    for u, (k0, k1) in enumerate(k_parts):
                        if mo == 1 and u == parts - 1:
                            pe.wait_ge(z_ready, KD * q + 1)
                            nc.tensor.matmul(bank[4][:, 0:n_tok], mean128[:], resid[:, 0, cols], start=True,
                                             stop=True).then_inc(shift_meaned, 1)
                        if mo == KD - 1 and u == parts - 1:
                            pe.wait_ge(totals_ready, (KD - 2) * (q + 1))
                            nc.tensor.matmul(bank[4][:, 0:n_tok], meanD[:], total[:, cols], start=True, stop=False)
                            nc.tensor.matmul(bank[5][:, 0:n_tok], meanD[:], total_sq[:, cols], start=True, stop=False)
                        multiply(ps, n0 + parts * mo + u, source, src_cols, k0, k1, u == 0, u == parts - 1, step,
                                 ready if mo == 0 else None)

                if parts == 3:
                    chunk(0)
                    chunk(1)
                    with pe.Fori(0, (KD - 4) // 2) as i:
                        chunk(2, i)
                        chunk(3, i)
                    chunk(KD - 2)
                    chunk(KD - 1)
                else:
                    for mo in range(KD):
                        chunk(mo)
                pe.wait_ge(z_ready, KD * (q + 1))
                nc.tensor.matmul(bank[4][:, 0:n_tok], meanD[:], resid[:, KD - 1, cols], start=False,
                                 stop=True).then_inc(stat_ready, 1)
                pe.wait_ge(sq_ready, KD * (q + 1))
                nc.tensor.matmul(bank[5][:, 0:n_tok], meanD[:], sq[:, (KD - 1) % 2, cols], start=False,
                                 stop=True).then_inc(stat_ready, 1)

            def ffn(f, n0, n_tok, gen):
                cols = tokens(n_tok)
                multiply_together([(bank[b][:, 0:n_tok], cols) for b in range(4)], n0, gen)

                def tile(t, step=0):
                    g = KF * f + t
                    if t >= SETS:
                        pe.wait_ge(mid_ready, step * SETS + (g - SETS + 1))
                    elif f:
                        pe.wait_ge(mid_ready, KF * f)
                    for half in range(2):
                        multiply(bank[2 * (t % SETS) + half][:, 0:n_tok], n0 + 2 * t + half, (x_hi, x_lo), cols,
                                 step=step)

                tile(2)
                tile(3)
                tile(4)
                with pe.Fori(0, (KF - 4) // SETS - 1) as i:
                    for t in range(5, 5 + SETS):
                        tile(t, i)
                tile(KF - 2)
                tile(KF - 1)
                out_projection(FFN_NORM[f], n0 + FFN_IN, K_PARTS, (mid_hi, mid_lo), (mid_ready, KF * f), n_tok)

            n_rows = consts.shape[1]
            pe.wait_ge(masks_set, 2)
            pe.wait_ge(rows_landed, 16 * 4)
            nc.tensor.transpose(bank[5][:, 0:n_rows], const_rows[0:n_rows, :], ident[0:n_rows, 0:n_rows]).then_inc(consts_turned, 1)
            pe.wait_ge(x_landed, 32)
            for k in range(KD):
                if k >= 2:
                    pe.wait_ge(h0_ready, k - 1)
                ps, chunk_cols = bank[6 + k % 2], slice(k * P, (k + 1) * P)
                nc.tensor.transpose(ps[:, 0:META], meta_tok[:, chunk_cols], ident[0:META, 0:META])
                for b in range(SEQ // P):
                    mm = nc.tensor.transpose(ps[:, META + b * P:META + (b + 1) * P], x_tok[:, b, chunk_cols], ident[:])
                mm.then_inc(x_turned, 1)
            pe.wait_ge(fills_done, 1)

            ffn(0, unit0["f0"], T, 0)

            n0 = unit0["conv"]
            every = slice(0, T)
            multiply_together([(bank[b][:, 0:T], every) for b in range(3)], n0, CONV_NORM)

            def conv_chunk(m, step=0):
                if m >= 2:
                    pe.wait_ge(yc_ready, step * 2 + (m - 1))
                for part in range(3):
                    multiply(bank[3 * (m % 2) + part][:, 0:T], n0 + 3 * m + part, (x_hi, x_lo), every, step=step)

            conv_chunk(1)
            with pe.Fori(0, KD // 2 - 1) as i:
                conv_chunk(2, i)
                conv_chunk(3, i)
            out_projection(CONV_NORM, n0 + 3 * KD, [(0, KU)], (yc_hi, yc_lo), (yc_ready, 0), T)

            ffn(1, unit0["f1"], T, 2)
            ffn(2, unit0["f2"], T, 3)

            n0 = unit0["gla"]
            main = tokens(SEQ)

            def logits():
                pe.wait_ge(gla_evac, 1)
                pe.wait_ge(gate_landed, 32)
                for c in range(NC + 1):
                    if c >= 2:
                        pe.wait_ge(logits_copied, c - 1)
                    nc.tensor.matmul(bank[4 + c % 2][0:rows(c), :], gzT[:, span(c)], gate_up[:], start=True,
                                     stop=True).then_inc(logits_made, 1)

            def cumulate(h):
                pe.wait_ge(log_a_ready, 2)
                if h >= 2:
                    pe.wait_ge(b_copied, h - 1)
                for c in range(NC + 1):
                    mm = nc.tensor.matmul(bank[6 + h % 2][:, span(c)], log_a[0:rows(c), c, h * P:(h + 1) * P],
                                          cum[0:rows(c), 0:rows(c)], start=True, stop=True)
                mm.then_inc(cum_made, 1)

            def turn_v(v):
                pe.wait_ge(gla_evac, 2 + 2 * HEADS + v)
                if v >= 1:
                    pe.wait_ge(v_tok_ready, v)
                nc.tensor.transpose(bank[2][0:META, 0:P], vT[:, v % 2, span(0)], ident[:])
                for c in range(1, NC + 1):
                    mm = nc.tensor.transpose(bank[5][0:CH, (c - 1) * P:c * P], vT[:, v % 2, span(c)], ident[:])
                mm.then_inc(v_turned, 1)

            def turn_k(h):
                pe.wait_ge(kst_ready, h + 1)
                if h >= 2:
                    pe.wait_ge(ms_copied, h - 1)
                for c in range(NC):
                    mm = nc.tensor.transpose(bank[4][0:rows(c), c * P:(c + 1) * P], k_st[:, h % 2, span(c)], ident[:])
                mm.then_inc(k_turned, 1)

            def scores(h):
                pe.wait_ge(decayed, 2 * h + 2)
                if h >= 1:
                    pe.wait_ge(o_copied, h)
                for c in range(1, NC + 1):
                    mm = nc.tensor.matmul(bank[3][0:CH, body(c)], kT[:, h, span(c)], q_pos[:, h, body(c)],
                                          start=True, stop=True)
                mm.then_inc(scores_made, 1)

            def outers(h):
                pe.wait_ge(k_tok_ready, h + 1)
                pe.wait_ge(v_tok_ready, VT * (h + 1))
                if h >= 1:
                    pe.wait_ge(state_ready, NC * h)
                for c in range(NC):
                    mm = nc.tensor.matmul(bank[6 + c // 2][:, (c % 2) * HV:(c % 2 + 1) * HV], k_tok[0:rows(c), h % 2, c, :],
                                          v_tok[0:rows(c), h % 2, c, :], start=True, stop=True)
                mm.then_inc(outer_made, 1)

            def outputs(h):
                pe.wait_ge(scores_masked, h + 1)
                pe.wait_ge(state_ready, NC * (h + 1))
                for vt in range(VT):
                    v_cols = slice(vt * P, (vt + 1) * P)
                    for c in range(1, NC + 1):
                        ps = bank[3][:, vt * SEQ + (c - 1) * CH:vt * SEQ + c * CH]
                        nc.tensor.matmul(ps, v_tok[:, h % 2, c, v_cols], sT[:, h % 2, body(c)], start=True, stop=False)
                        mm = nc.tensor.matmul(ps, state[:, c - 1, v_cols], qT[:, h, body(c)], start=False, stop=True)
                mm.then_inc(o_made, 1)

            def mean_square(h):
                pe.wait_ge(o_squared, h + 1)
                pe.wait_ge(k_tok_ready, min(h + 2, HEADS))
                if h >= 1:
                    pe.wait_ge(ms_copied, h)
                for vt in range(VT):
                    mm = nc.tensor.matmul(bank[4][:, 0:SEQ], meanV[:], o_sq[:, vt, :], start=vt == 0, stop=vt == VT - 1)
                mm.then_inc(ms_made, 1)

            multiply_together([(bank[b][:, 0:T], every) for b in range(4)], n0, GLA_NORM)
            for j in range(4, GLA_TILES):
                pe.wait_ge(gla_evac, j - 3 if j < 6 else j - 1)
                short = HEADS < j <= 2 * HEADS or j > 2 * HEADS + KD
                cols = main if short else every
                multiply(bank[j % 2][:, 0:SEQ if short else T], n0 + j, (x_hi, x_lo), cols)
                if j == 4:
                    logits()
                if j == 8:
                    cumulate(0)
                    cumulate(1)
                if j in (9, 10):
                    cumulate(j - 7)
                if 10 <= j < 10 + KD:
                    turn_v(j - 10)
                h, phase = (j - 11) // 2, (j - 11) % 2
                if j >= 11 and phase == 0:
                    if 0 <= h - 1 < HEADS:
                        outputs(h - 1)
                    if h < HEADS:
                        turn_k(h)
                        scores(h)
                if j >= 11 and phase == 1:
                    if h < HEADS:
                        outers(h)
                    if 0 <= h - 1 < HEADS:
                        mean_square(h - 1)
            out_projection(GLA_NORM, n0 + GLA_TILES, [(0, KU)], (y_hi, y_lo), (y_ready, 0), SEQ)

            ffn(3, unit0["f3"], SEQ, 5)

            for k in range(KD):
                pe.wait_ge(h_ready, KD * LAST_NORM + k + 1)
                for b in range(SEQ // P):
                    mm = nc.tensor.transpose(bank[2 * (k // (KD // 2)) + b][:, (k % (KD // 2)) * P:(k % (KD // 2) + 1) * P],
                                             resid[:, k, META + b * P:META + (b + 1) * P], ident[:])
                if k % (KD // 2) == KD // 2 - 1:
                    mm.then_inc(out_turned, 1)


_INS = ["x", "meta_tokens", "ln_gain", "ln_bias", "ffn_w_in", "ffn_w_out", "conv_w_in", "conv_w", "conv_w_out",
        "gla_w_in", "gla_w_gate_up", "gla_b_gate", "gla_norm_w", "gla_w_out"]
_OUTS = [((1, 256, 1024), "float32")]


def kernel(**inputs):
    import numpy as _np
    import concourse.bacc as _bacc
    from concourse import mybir as _mybir
    from concourse.bass_utils import run_bass_kernel_spmd as _run

    nc = _bacc.Bacc("TRN2", target_bir_lowering=False, num_devices=1)
    arrays, args = {}, []
    for name in _INS:
        a = _np.ascontiguousarray(inputs[name])
        arrays[f"in_{name}_dram"] = a
        args.append(nc.dram_tensor(f"in_{name}_dram", a.shape, _mybir.dt.from_np(a.dtype), kind="ExternalInput").ap())
    for i, (shape, dtype) in enumerate(_OUTS):
        dt = _mybir.dt.from_np(_np.dtype(dtype))
        args.append(nc.dram_tensor(f"out_{i}_dram", shape, dt, kind="ExternalOutput").ap())
    hybrid_trunk(nc, *args)
    r = _run(nc, [arrays], core_ids=[0])
    got = tuple(r.results[0][f"out_{i}_dram"] for i in range(len(_OUTS)))
    return got[0]
```

```python
from contextlib import ExitStack

import concourse.bass as bass
from concourse import mybir

F32 = mybir.dt.float32
F32R = mybir.dt.float32r
ALU = mybir.AluOpType
ACT = mybir.ActivationFunctionType

P = 128
LN_EPS = 1e-5
RMS_EPS = 1e-6
RING = 6
KU = 8
WARM = (3, 3, 4, 8)


def hybrid_trunk(nc, x, meta_tokens, ln_gain, ln_bias, ffn_w_in, ffn_w_out, conv_w_in, conv_w,
                 conv_w_out, gla_w_in, gla_w_gate_up, gla_b_gate, gla_norm_w, gla_w_out, out):
    _, SEQ, D = x.shape
    META = meta_tokens.shape[0]
    DEPTH = ln_gain.shape[0]
    F = ffn_w_out.shape[2]
    TAPS = conv_w.shape[1]
    RANK, DK = gla_w_gate_up.shape[1:]
    T = META + SEQ
    KD = D // P
    KF = F // P
    HEADS = DK // P
    VT = KD // HEADS
    HV = VT * P
    CH = 64
    NC = SEQ // CH
    KT0 = META + (NC - 1) * CH
    ALPHA = (2.0 * DEPTH) ** 0.25
    SETS = 3
    assert D == KU * P and META < CH // 2 and gla_norm_w.shape[1] == HV and DEPTH == 2

    FFN_IN, FFN_OUT = 2 * KF, 3 * KD
    K_PARTS = [(0, 8), (8, 16), (16, KF)]
    GLA_TILES = 1 + KD // 2 + KD // 2 + KD + KD
    unit0, at = {}, 0
    for name, count in [("f0", FFN_IN + FFN_OUT), ("conv", 4 * KD), ("f1", FFN_IN + FFN_OUT),
                        ("f2", FFN_IN + FFN_OUT), ("gla", GLA_TILES + KD), ("f3", FFN_IN + FFN_OUT)]:
        unit0[name] = at
        at += count
    UNITS = at
    CONV_PARTS = (1, 2, 0)
    FFN_NORM = [0, 2, 3, 5]
    CONV_NORM, GLA_NORM = 1, 4
    LAST_NORM = 3 * DEPTH - 1

    ctx = ExitStack()
    with ctx:
        def sb(name, shape, dt=F32):
            return ctx.enter_context(nc.sbuf_tensor(name, shape, dt))

        def sem(name):
            return ctx.enter_context(nc.semaphore(name))

        raw = sb("raw_weights", [P, RING, KU * P])
        w_hi = sb("weights_hi", [P, RING, KU * P], F32R)
        w_lo = sb("weights_lo", [P, RING, KU * P], F32R)
        x_hi = sb("x_hi", [P, KD, T], F32R)
        x_lo = sb("x_lo", [P, KD, T], F32R)
        resid = sb("resid", [P, KD, T])
        consts = sb("consts", [P, 6 * KD * 2 + TAPS * KD + VT])
        ident = sb("ident", [P, P])
        z0_hi = sb("z0_hi", [P, T], F32R)
        mean128 = sb("mean128", [P, P], F32R)
        meanD = sb("meanD", [P, P])
        meanV = sb("meanV", [P, P])
        eps = sb("eps", [P, 2])
        table_warm = sb("table_warm", [P, 1])
        shift = sb("shift", [P, T])
        total = sb("total", [P, T])
        total_sq = sb("total_sq", [P, T])
        sq = sb("sq", [P, 2, T])
        mean = sb("mean", [P, T])
        mean_sq = sb("mean_sq", [P, T])
        var = sb("var", [P, T])
        std = sb("std", [P, T])
        rstd = sb("rstd", [P, T])
        scaled = sb("scaled", [P, 3, T])
        h_f = sb("h_f", [P, 3, T])
        silu_g = sb("silu_g", [P, SETS, T])
        prod = sb("prod", [P, SETS, T])

        with ExitStack() as inner:
            mid_hi = inner.enter_context(nc.sbuf_tensor("mid_hi", [P, KF, T], F32R))
            mid_lo = inner.enter_context(nc.sbuf_tensor("mid_lo", [P, KF, T], F32R))
        with ExitStack() as first:
            x_tok = first.enter_context(nc.sbuf_tensor("x_tok", [P, SEQ // P, D], F32))
            meta_tok = first.enter_context(nc.sbuf_tensor("meta_tok", [META, D], F32))
            const_rows = first.enter_context(nc.sbuf_tensor("const_rows", [P, P], F32))
        with ExitStack() as final:
            out_tok = final.enter_context(nc.sbuf_tensor("out_tok", [P, SEQ // P, D], F32))
        with ExitStack() as conv:
            cu = conv.enter_context(nc.sbuf_tensor("cu", [P, 2, TAPS - 1 + T], F32))
            u_sb = conv.enter_context(nc.sbuf_tensor("u_sb", [P, 2, T], F32))
            conv_t = conv.enter_context(nc.sbuf_tensor("conv_t", [P, 2, T], F32))
            yc_hi = conv.enter_context(nc.sbuf_tensor("yc_hi", [P, KD, T], F32R))
            yc_lo = conv.enter_context(nc.sbuf_tensor("yc_lo", [P, KD, T], F32R))
        gla = ctx.enter_context(ExitStack())

        def gb(name, shape, dt=F32):
            return gla.enter_context(nc.sbuf_tensor(name, shape, dt))

        y_hi = gb("y_hi", [P, KD, SEQ], F32R)
        y_lo = gb("y_lo", [P, KD, SEQ], F32R)
        kT = gb("kT", [P, HEADS, T])
        qT = gb("qT", [P, HEADS, SEQ])
        q_pos = gb("q_pos", [P, HEADS, SEQ])
        k_st = gb("k_st", [P, 2, KT0])
        BLOCKS = 1 + NC // 2
        gate_area = gb("gate_area", [P, 2, KD * SEQ])
        log_a = gate_area[:, 0, 0:BLOCKS * DK].rearrange("p (b n) -> p b n", b=BLOCKS)
        soft = gate_area[:, 1, 0:BLOCKS * DK].rearrange("p (b n) -> p b n", b=BLOCKS)
        o_sb = gate_area[:, 0, 0:KD * SEQ].rearrange("p (m t) -> p m t", m=KD)
        silu_out = gate_area[:, 1, 0:KD * SEQ].rearrange("p (m t) -> p m t", m=KD)
        b_sb = h_f
        d_ref = scaled[:, :, 0:SEQ]
        d_last = gb("d_last", [P, 2, KT0])
        e_buf = silu_g[:, :, 0:SEQ]
        e_last = gb("e_last", [P, KT0])
        decay = gb("decay", [P, HEADS, NC])
        vT = prod[:, 0:2, :]
        v_tok = gb("v_tok", [P, 2, BLOCKS, HV])
        k_tok = gb("k_tok", [P, 2, BLOCKS, P])
        sT = gb("sT", [P, 2, SEQ])
        state = gb("state", [P, NC, HV])
        o_sq = gb("o_sq", [P, VT, SEQ])
        rms = gb("rms", [P, SEQ])
        y_t = q_pos[:, 0:2, :]
        gzT = sb("gzT", [RANK + 1, T])
        gate_up = sb("gate_up", [RANK + 1, DK])
        cum = sb("cum", [P, P])
        pick = sb("pick", [P, P])

        bank = [ctx.enter_context(nc.psum_tensor(f"bank{i}", [P, 512], F32)) for i in range(8)]

        raw_landed = [sem(f"raw_landed{i}") for i in range(RING)]
        hi_split, lo_split, unit_used = sem("hi_split"), sem("lo_split"), sem("unit_used")
        rows_landed, gate_landed = sem("rows_landed"), sem("gate_landed")
        meta_landed, x_landed = sem("meta_landed"), [sem("x_landed0"), sem("x_landed1")]
        ident_zeroed, masks_set, fills_done = sem("ident_zeroed"), sem("masks_set"), sem("fills_done")
        consts_turned, consts_ready = sem("consts_turned"), sem("consts_ready")
        x_turned, h0_ready = sem("x_turned"), sem("h0_ready")
        xhi_ready, xlo_ready, resid_ready, resid_late = sem("xhi_ready"), sem("xlo_ready"), sem("resid_ready"), sem("resid_late")
        silu_ready, prod_ready = sem("silu_ready"), sem("prod_ready")
        midhi_ready, mid_ready = sem("midhi_ready"), sem("mid_ready")
        z_ready, shift_meaned, shift_copied = sem("z_ready"), sem("shift_meaned"), sem("shift_copied")
        shifted, sq_ready, total_ready, totals_ready = sem("shifted"), sem("sq_ready"), sem("total_ready"), sem("totals_ready")
        stat_ready, mean_copied, meansq_ready = sem("stat_ready"), sem("mean_copied"), sem("meansq_ready")
        z_summed, sq_summed = sem("z_summed"), sem("sq_summed")
        mean_filled, z0_rounded = sem("mean_filled"), sem("z0_rounded")
        first_centred = sem("first_centred")
        centred, var_ready, std_ready, rstd_ready = sem("centred"), sem("var_ready"), sem("std_ready"), sem("rstd_ready")
        scaled_ready, h_ready = sem("scaled_ready"), sem("h_ready")
        pad_zeroed, u_copied, conv_step, yc_ready = sem("pad_zeroed"), sem("u_copied"), sem("conv_step"), sem("yc_ready")
        gz_ones, gla_evac = sem("gz_ones"), sem("gla_evac")
        logits_made, logits_copied, logits_folded, soft_step, log_a_ready = sem("logits_made"), sem("logits_copied"), sem("logits_folded"), sem("soft_step"), sem("log_a_ready")
        pick_zeroed, alpha_applied, shift_off = sem("pick_zeroed"), sem("alpha_applied"), sem("shift_off")
        cum_made, b_copied, diffs_ready = sem("cum_made"), sem("b_copied"), sem("diffs_ready")
        exps_ready, kst_ready, decayed = sem("exps_ready"), sem("kst_ready"), sem("decayed")
        v_turned, v_tok_ready = sem("v_turned"), sem("v_tok_ready")
        k_turned, k_tok_ready = sem("k_turned"), sem("k_tok_ready")
        scores_made, scores_copied, scores_masked = sem("scores_made"), sem("scores_copied"), sem("scores_masked")
        outer_made, state_ready = sem("outer_made"), sem("state_ready")
        o_made, o_copied, o_squared = sem("o_made"), sem("o_copied"), sem("o_squared")
        ms_made, rms_root, rms_ready, rms_spread = sem("ms_made"), sem("rms_root"), sem("rms_ready"), sem("rms_spread")
        o_scaled = sem("o_scaled")
        y_step, yhi_ready, y_ready = sem("y_step"), sem("yhi_ready"), sem("y_ready")
        out_turned, out_copied, last_copied, out_stored = sem("out_turned"), sem("out_copied"), sem("last_copied"), sem("out_stored")

        RMS_BANKS = (6, 7, 4, 5)
        Y_CHUNKS = {21: (0, 1), 22: (2, 3), 23: (4, 5), 24: (6, 7)}

        def ln_gain_col(q, k):
            return consts[:, q * KD + k:q * KD + k + 1]

        def ln_bias_col(q, k):
            return consts[:, (6 + q) * KD + k:(6 + q) * KD + k + 1]

        def conv_col(tap, m):
            return consts[:, bass.ds((12 + tap) * KD + m, 1)]

        def norm_col(vt):
            return consts[:, (12 + TAPS) * KD + vt:(12 + TAPS) * KD + vt + 1]

        def tokens(n):
            return slice(T - n, T)

        def span(c):
            return slice(0, META) if c == 0 else slice(META + (c - 1) * CH, META + c * CH)

        def blk(c):
            return 0 if c == 0 else 1 + (c - 1) // 2

        def rows(c):
            return slice(0, META) if c == 0 else slice((c - 1) % 2 * CH, ((c - 1) % 2 + 1) * CH)

        def outer_tile(c):
            i, first = [(6, 0), (6, HV), (4, 0), (7, 0)][c]
            return bank[i][:, first:first + HV]

        def body(c):
            return slice((c - 1) * CH, c * CH)

        block = ctx.enter_context(nc.Block())

        @block.sync
        def _(sp):
            def load(n, source, step=0):
                if n >= RING:
                    sp.wait_ge(lo_split, n + 1 - RING + step * RING)
                elif n in (1, 2):
                    sp.wait_ge(x_landed[n - 1], 16)
                cols = source.shape[-1]
                dst = raw[:, n % RING, :].rearrange("p (k c) -> p k c", c=P)[:, 0:source.shape[1], 0:cols]
                sp.dma_start(dst, source).then_inc(raw_landed[n % RING], 16)

            def columns(w):
                return w.rearrange("(k p) n -> p k n", p=P)

            def load_ffn(f, n0):
                w_in = columns(ffn_w_in[f // 2, f % 2])
                w_out = columns(ffn_w_out[f // 2, f % 2])

                def tile_pair(n, t, step=0):
                    load(n, w_in[:, :, bass.ds(t * P, P)], step)
                    load(n + 1, w_in[:, :, bass.ds(F + t * P, P)], step)

                for t in range(4):
                    tile_pair(n0 + 2 * t, t)
                with sp.Fori(0, (KF - 4) // SETS) as i:
                    for j in range(SETS):
                        tile_pair(n0 + 8 + 2 * j, i * SETS + (4 + j), i)
                with sp.Fori(0, KD // 2) as i:
                    for j in range(2):
                        for u, (k0, k1) in enumerate(K_PARTS):
                            load(n0 + FFN_IN + 3 * j + u, w_out[:, k0:k1, bass.ds(i * 2 * P + j * P, P)], i)

            sp.dma_start(x_tok[:, :, 0:D // 2], x[0].rearrange("(b p) d -> p b d", p=P)[:, :, 0:D // 2]).then_inc(x_landed[0], 16)
            load_ffn(0, unit0["f0"])
            n = unit0["conv"]
            w = columns(conv_w_in[0])
            for m in range(KD):
                for u, part in enumerate(CONV_PARTS):
                    load(n + 3 * m + u, w[:, :, part * D + m * P:part * D + (m + 1) * P])
            w = columns(conv_w_out[0])
            for m in range(KD):
                load(n + 3 * KD + m, w[:, :, m * P:(m + 1) * P])
            load_ffn(1, unit0["f1"])
            load_ffn(2, unit0["f2"])
            n = unit0["gla"]
            w = columns(gla_w_in[0])
            load(n, w[:, :, 2 * DK + 2 * D:2 * DK + 2 * D + RANK])
            for m in range(GLA_TILES - 1):
                c0 = DK + m * P if m < HEADS else (m - HEADS) * P if m < 2 * HEADS else m * P
                load(n + 1 + m, w[:, :, c0:c0 + P])
            w = columns(gla_w_out[0])
            for m in range(KD):
                load(n + GLA_TILES + m, w[:, :, m * P:(m + 1) * P])
            load_ffn(3, unit0["f3"])
            for part in range(3):
                sp.wait_ge(out_copied, part + 1)
                b, cols = part % 2, slice(part // 2 * D // 2, (part // 2 + 1) * D // 2)
                sp.dma_start(out[0, b * P:(b + 1) * P, cols], out_tok[:, b, cols]).then_inc(out_stored, 16)
            sp.wait_ge(out_stored, 16 * 4)

        @block.gpsimd
        def _(pool):
            nc.gpsimd.memset(ident[:], 0.0).then_inc(ident_zeroed, 1)
            pool.wait_ge(ident_zeroed, 1)
            nc.gpsimd.affine_select(out=ident[:], in_=ident[:], compare_op=ALU.not_equal, fill=1.0, base=0,
                                    pattern=[[-1, P]], channel_multiplier=1).then_inc(masks_set, 1)
            row = 0
            for source in (ln_gain.rearrange("l s (k p) -> (l s k) p", p=P),
                           ln_bias.rearrange("l s (k p) -> (l s k) p", p=P),
                           conv_w.rearrange("l s (k p) -> (l s k) p", p=P),
                           gla_norm_w.rearrange("l (k p) -> (l k) p", p=P)):
                pool.dma_start(const_rows[row:row + source.shape[0], :], source).then_inc(rows_landed, 16)
                row += source.shape[0]
            for n in range(2):
                pool.wait_ge(hi_split, n + 1)
                if n:
                    pool.wait_ge(lo_split, n)
                nc.gpsimd.tensor_tensor(w_lo[:, n, :], raw[:, n, :], w_hi[:, n, :].bitcast(F32),
                                        ALU.subtract).then_inc(lo_split, 1)
            pool.dma_start(gate_up[0:RANK, :], gla_w_gate_up[0]).then_inc(gate_landed, 16)
            pool.dma_start(gate_up[RANK:RANK + 1, :], gla_b_gate).then_inc(gate_landed, 16)
            nc.gpsimd.memset(cum[:], 1.0 / 16.0).then_inc(ident_zeroed, 1)
            nc.gpsimd.memset(pick[:], 0.0).then_inc(pick_zeroed, 1)
            pool.wait_ge(ident_zeroed, 2)
            pool.wait_ge(masks_set, 1)
            nc.gpsimd.affine_select(out=cum[:], in_=cum[:], compare_op=ALU.is_ge, fill=0.0, base=0,
                                    pattern=[[1, P]], channel_multiplier=-1).then_inc(masks_set, 1)
            pool.wait_ge(masks_set, 2)
            nc.gpsimd.memset(cum[0:CH, CH:P], 0.0).then_inc(masks_set, 1)
            pool.wait_ge(pick_zeroed, 1)
            for h in range(HEADS):
                pool.wait_ge(masks_set, h + 3)
                first_row = pick[h * 32:(h + 1) * 32, :]
                nc.gpsimd.affine_select(out=first_row, in_=first_row, compare_op=ALU.not_equal, fill=1.0, base=0,
                                        pattern=[[0, P]], channel_multiplier=1).then_inc(masks_set, 1)
            pool.wait_ge(masks_set, 3 + HEADS)

            def add_up(q, n_tok):
                cols = tokens(n_tok)

                def chunk(mo, step=0):
                    pool.wait_ge(z_ready, step * 2 + (KD * q + mo + 1))
                    if mo >= 2:
                        pool.wait_ge(total_ready, step * 2 + ((KD - 2) * q + mo - 1))
                    before = resid[:, 0:1, cols] if mo == 1 else total[:, cols]
                    nc.gpsimd.tensor_tensor(total[:, cols], before, resid[:, bass.ds(step * 2 + mo, 1), cols],
                                            ALU.add).then_inc(total_ready, 1)
                    pool.wait_ge(sq_ready, step * 2 + (KD * q + mo + 1))
                    if mo >= 2:
                        pool.wait_ge(totals_ready, step * 2 + ((KD - 2) * q + mo - 1))
                    nc.gpsimd.tensor_tensor(total_sq[:, cols], total_sq[:, cols], sq[:, mo % 2, cols],
                                            ALU.add).then_inc(totals_ready, 1)

                chunk(1)
                with pool.Fori(0, (KD - 4) // 2) as i:
                    chunk(2, i)
                    chunk(3, i)
                chunk(KD - 2)

            def centre(q, n_tok):
                cols = tokens(n_tok)
                pool.wait_ge(mean_copied, q + 1)
                for k in range(1, KD):
                    nc.gpsimd.tensor_tensor(resid[:, k, cols], resid[:, k, cols], mean[:, cols],
                                            ALU.subtract).then_inc(centred, 1)

            def next_residual(q, n_tok):
                cols = tokens(n_tok)
                for k in range(KD // 2, KD):
                    pool.wait_ge(h_ready, KD * q + k + 1)
                    nc.gpsimd.tensor_scalar(resid[:, k, cols], h_f[:, k % 3, cols], ALPHA, None,
                                            ALU.mult).then_inc(resid_late, 1)

            for q in range(GLA_NORM):
                add_up(q, T)
                centre(q, T)
                next_residual(q, T)
            def apply_decays(h):
                pool.wait_ge(exps_ready, 5 * h + 1)
                pool.wait_ge(gla_evac, 1 + HEADS)
                if h >= 2:
                    pool.wait_ge(k_turned, h - 1)
                nc.gpsimd.tensor_tensor(k_st[:, h % 2, :], kT[:, h, 0:KT0], e_last[:], ALU.mult).then_inc(kst_ready, 1)
                pool.wait_ge(exps_ready, 5 * h + 4)
                pool.wait_ge(gla_evac, 1 + 2 * HEADS)
                nc.gpsimd.tensor_tensor(q_pos[:, h, :], qT[:, h, :], e_buf[:, 0, :], ALU.mult).then_inc(decayed, 1)
                pool.wait_ge(kst_ready, h + 1)
                nc.gpsimd.tensor_tensor(kT[:, h, META:T], kT[:, h, META:T], e_buf[:, 1, :], ALU.mult)
                pool.wait_ge(decayed, 2 * h + 1)
                nc.gpsimd.tensor_tensor(qT[:, h, :], qT[:, h, :], e_buf[:, 2, :], ALU.mult).then_inc(decayed, 1)

            def mask_scores(h):
                if h:
                    pool.wait_ge(scores_masked, 2 * h)
                pool.wait_ge(scores_copied, h + 1)
                s = sT[:, h % 2, :].rearrange("p (b i) -> p b i", i=P)
                nc.gpsimd.affine_select(out=s, in_=s, compare_op=ALU.is_ge, fill=0.0, base=0,
                                        pattern=[[0, NC // 2], [1, P]], channel_multiplier=-1).then_inc(scores_masked, 1)
                pool.wait_ge(scores_masked, 2 * h + 1)
                nc.gpsimd.memset(s[0:CH, :, CH:P], 0.0).then_inc(scores_masked, 1)
            def gate_output(m):
                pool.wait_ge(gla_evac, 2 + 2 * HEADS + KD + m)
                pool.wait_ge(o_scaled, m + 1)
                if m >= 2:
                    pool.wait_ge(y_ready, m - 1)
                nc.gpsimd.tensor_tensor(y_t[:, m % 2, :], o_sb[:, m, :], silu_out[:, m, :], ALU.mult).then_inc(y_step, 1)

            for h in range(HEADS):
                apply_decays(h)
                mask_scores(h)
            for m in range(KD):
                gate_output(m)
            add_up(GLA_NORM, SEQ)
            centre(GLA_NORM, SEQ)
            next_residual(GLA_NORM, SEQ)
            add_up(LAST_NORM, SEQ)
            centre(LAST_NORM, SEQ)

        @block.scalar
        def _(act):
            def split_hi(n, step=0):
                if n >= RING:
                    act.wait_ge(unit_used, n + 1 - RING + step * RING)
                act.wait_ge(raw_landed[n % RING], (step + (n // RING + 1)) * 16)
                nc.scalar.activation(w_hi[:, n % RING, :], raw[:, n % RING, :], ACT.Copy).then_inc(hi_split, 1)

            def square_chunk(q, mo, n_tok, step=0):
                cols = tokens(n_tok)
                if mo == 0:
                    act.wait_ge(shifted, q + 1)
                    nc.scalar.activation(total_sq[:, cols], resid[:, 0, cols], ACT.Square).then_inc(sq_ready, 1)
                    return
                act.wait_ge(z_ready, step * 2 + (KD * q + mo + 1))
                if mo >= 2:
                    act.wait_ge(totals_ready, step * 2 + ((KD - 2) * q + mo - 1))
                elif q:
                    act.wait_ge(stat_ready, 2 * q)
                nc.scalar.activation(sq[:, mo % 2, cols], resid[:, bass.ds(step * 2 + mo, 1), cols],
                                     ACT.Square).then_inc(sq_ready, 1)

            def normalise(q, n_tok, late):
                def split_hi_late(i):
                    if i < len(late):
                        split_hi(late[i] + RING)

                cols = tokens(n_tok)
                act.wait_ge(stat_ready, 2 * q + 1)
                nc.scalar.activation(mean_sq[:, cols], bank[4][:, 0:n_tok], ACT.Square).then_inc(meansq_ready, 1)
                nc.scalar.activation(mean[:, cols], bank[4][:, 0:n_tok], ACT.Copy).then_inc(mean_copied, 1)
                act.wait_ge(var_ready, q + 1)
                nc.scalar.activation(std[:, cols], var[:, cols], ACT.Sqrt, bias=eps[:, 0:1]).then_inc(std_ready, 1)
                for k in range(KD):
                    act.wait_ge(scaled_ready, KD * q + k + 1)
                    if q == LAST_NORM:
                        nc.scalar.activation(resid[:, k, cols], scaled[:, k % 3, cols], ACT.Identity,
                                             bias=ln_bias_col(q, k)).then_inc(h_ready, 1)
                        continue
                    nc.scalar.activation(x_hi[:, k, cols], scaled[:, k % 3, cols], ACT.Identity,
                                         bias=ln_bias_col(q, k)).then_inc(xhi_ready, 1)
                    if k >= 3:
                        act.wait_ge(xlo_ready, KD * (q + 1) + k - 2)
                    if 0 <= k - 3 < KD // 2:
                        act.wait_ge(resid_ready, KD // 2 * q + k - 2)
                    if k - 3 >= KD // 2:
                        act.wait_ge(resid_late, KD // 2 * q + (k - 2 - KD // 2))
                    nc.scalar.activation(h_f[:, k % 3, cols], scaled[:, k % 3, cols], ACT.Identity,
                                         bias=ln_bias_col(q, k)).then_inc(h_ready, 1)
                    if 1 <= k <= KD // 2:
                        act.wait_ge(h_ready, KD * q + k)
                        nc.scalar.mul(resid[:, k - 1, cols], h_f[:, (k - 1) % 3, cols], ALPHA).then_inc(resid_ready, 1)
                    if k in (4, 6):
                        split_hi_late((k - 4) // 2)
                if q == LAST_NORM:
                    act.wait_ge(out_turned, 2)
                    nc.scalar.activation(out_tok[:, 1, D // 2:], bank[3][:], ACT.Copy).then_inc(last_copied, 1)
                    act.wait_ge(last_copied, 1)
                    act.dma_start(out[0, P:, D // 2:], out_tok[:, 1, D // 2:]).then_inc(out_stored, 16)

            def out_projection(q, n0, parts, n_tok):
                def chunk(mo, step=0):
                    n = n0 + parts * mo
                    if mo == KD - 1:
                        if parts == 3 and n + RING < UNITS:
                            split_hi(n + RING)
                        nc.scalar.activation(table_warm[:], eps[:, 0:1], ACT.Sqrt)
                        square_chunk(q, mo, n_tok)
                        normalise(q, n_tok, range(n + parts // 2, n + parts) if q != LAST_NORM else ())
                        return
                    for u in range(parts - 1):
                        if n + u + RING < UNITS:
                            split_hi(n + u + RING, step)
                    if n + parts - 1 + RING < UNITS:
                        split_hi(n + parts - 1 + RING, step)
                    if mo == 0:
                        act.wait_ge(z_ready, KD * q + 1)
                        nc.scalar.activation(z0_hi[:, tokens(n_tok)], resid[:, 0, tokens(n_tok)],
                                             ACT.Copy).then_inc(z0_rounded, 1)
                    if mo == 1:
                        square_chunk(q, 0, n_tok)
                    if mo >= 1:
                        square_chunk(q, mo, n_tok, step)
                if parts == 3:
                    chunk(0)
                    chunk(1)
                    with act.Fori(0, (KD - 4) // 2) as i:
                        chunk(2, i)
                        chunk(3, i)
                    chunk(KD - 2)
                    chunk(KD - 1)
                else:
                    for mo in range(KD):
                        chunk(mo)

            def ffn(f, n0, n_tok):
                cols = tokens(n_tok)

                def silu(t, step=0):
                    g = KF * f + t
                    act.wait_ge(unit_used, step * RING + (n0 + 2 * t + 1))
                    if g >= SETS:
                        act.wait_ge(mid_ready, step * SETS + (g - SETS + 1))
                    nc.scalar.activation(silu_g[:, t % SETS, cols], bank[2 * (t % SETS)][:, 0:n_tok],
                                         ACT.Silu).then_inc(silu_ready, 1)

                def tile(t, step=0):
                    n = n0 + 2 * t
                    split_hi(n + RING, step)
                    silu(t, step)
                    split_hi(n + 1 + RING, step)

                silu(0)
                split_hi(n0 + RING)
                silu(1)
                for u in range(1, 4):
                    split_hi(n0 + u + RING)
                for t in range(2, 2 + SETS):
                    tile(t)
                with act.Fori(0, (KF - 4) // SETS - 1) as i:
                    for t in range(2 + SETS, 2 + 2 * SETS):
                        tile(t, i)
                tile(KF - 2)
                tile(KF - 1)
                out_projection(FFN_NORM[f], n0 + FFN_IN, 3, n_tok)

            act.dma_start(meta_tok[:], meta_tokens).then_inc(meta_landed, 16)
            act.dma_start(x_tok[:, :, D // 2:], x[0].rearrange("(b p) d -> p b d", p=P)[:, :, D // 2:]).then_inc(x_landed[1], 16)
            split_hi(0)
            for k in range(KD):
                act.wait_ge(h0_ready, k + 1)
                nc.scalar.activation(x_hi[:, k, :], resid[:, k, :], ACT.Copy).then_inc(xhi_ready, 1)
                if k == 3:
                    split_hi(1)
            for n in range(2, RING):
                split_hi(n)
            act.wait_ge(consts_turned, 1)
            nc.scalar.activation(consts[:], bank[5][:, 0:consts.shape[1]], ACT.Copy).then_inc(consts_ready, 1)
            act.wait_ge(xlo_ready, KD)
            nc.scalar.mul(resid[:], resid[:], ALPHA).then_inc(alpha_applied, 1)
            act.wait_ge(consts_ready, 1)
            act.wait_ge(fills_done, 1)

            ffn(0, unit0["f0"], T)

            n0 = unit0["conv"]

            def copy_u(m, step=0):
                act.wait_ge(unit_used, step * RING + (n0 + 3 * m + 2))
                if m >= 2:
                    act.wait_ge(yc_ready, step * 2 + (m - 1))
                nc.scalar.activation(u_sb[:, m % 2, :], bank[3 * (m % 2) + 1][:, 0:T], ACT.Copy).then_inc(u_copied, 1)

            def conv_chunk(m, step=0):
                n = n0 + 3 * m
                split_hi(n + RING, step)
                copy_u(m, step)
                split_hi(n + 1 + RING, step)
                split_hi(n + 2 + RING, step)

            conv_chunk(0)
            conv_chunk(1)
            with act.Fori(0, KD // 2 - 1) as i:
                conv_chunk(2, i)
                conv_chunk(3, i)
            out_projection(CONV_NORM, n0 + 3 * KD, 1, T)

            ffn(1, unit0["f1"], T)
            ffn(2, unit0["f2"], T)

            n0 = unit0["gla"]
            act.wait_ge(gz_ones, 1)

            def gla_tile(j):
                act.wait_ge(unit_used, n0 + j + 1)
                ps = bank[j if j < 4 else j % 2]
                if j == 0:
                    nc.scalar.activation(gzT[0:RANK, :], ps[0:RANK, 0:T], ACT.Copy).then_inc(gla_evac, 1)
                elif j <= HEADS:
                    nc.scalar.activation(kT[:, j - 1, :], ps[:, 0:T], ACT.Copy).then_inc(gla_evac, 1)
                elif j <= 2 * HEADS:
                    nc.scalar.mul(qT[:, j - 1 - HEADS, :], ps[:, 0:SEQ], float(P) ** -0.5).then_inc(gla_evac, 1)
                elif j <= 2 * HEADS + KD:
                    v = j - 1 - 2 * HEADS
                    if v >= 2:
                        act.wait_ge(v_turned, v - 1)
                    nc.scalar.activation(vT[:, v % 2, :], ps[:, 0:T], ACT.Copy).then_inc(gla_evac, 1)
                else:
                    m = j - 1 - 2 * HEADS - KD
                    if m == 0:
                        act.wait_ge(log_a_ready, 2)
                    nc.scalar.activation(silu_out[:, m, :], ps[:, 0:SEQ], ACT.Silu).then_inc(gla_evac, 1)
                if j < GLA_TILES - 1:
                    split_hi(n0 + j + RING)

            def softplus(stage):
                areas = [soft[0:META, 0, :], soft[:, 1:, :]]
                if stage == 0:
                    act.wait_ge(logits_folded, BLOCKS)
                    for a in areas:
                        nc.scalar.activation(a, a, ACT.Exp).then_inc(soft_step, 1)
                else:
                    act.wait_ge(soft_step, 2)
                    for a in areas:
                        nc.scalar.activation(a, a, ACT.Ln, bias=1.0).then_inc(soft_step, 1)

            def copy_b(h):
                act.wait_ge(cum_made, h + 1)
                if h == 0:
                    act.wait_ge(resid_late, KD // 2 * GLA_NORM)
                if h >= 3:
                    act.wait_ge(exps_ready, 5 * (h - 2))
                    act.wait_ge(diffs_ready, 3 * (h - 2))
                nc.scalar.activation(b_sb[:, h % 3, :], bank[6 + h % 2][:, 0:T], ACT.Copy).then_inc(b_copied, 1)

            def decays(h):
                act.wait_ge(diffs_ready, 3 * h + 3)
                if h >= 1:
                    act.wait_ge(decayed, 2 * h)
                nc.scalar.activation(e_last[:], d_last[:, h % 2, :], ACT.Exp, scale=-1.0).then_inc(exps_ready, 1)
                nc.scalar.activation(e_buf[:, 0, :], d_ref[:, h % 3, :], ACT.Exp).then_inc(exps_ready, 1)
                nc.scalar.activation(e_buf[:, 1, :], d_ref[:, h % 3, :], ACT.Exp, scale=-1.0).then_inc(exps_ready, 1)
                nc.scalar.activation(e_buf[:, 2, :], b_sb[:, h % 3, META:T], ACT.Exp).then_inc(exps_ready, 1)
                nc.scalar.activation(decay[:, h, :], b_sb[:, h % 3, META - 1:KT0:CH], ACT.Exp).then_inc(exps_ready, 1)

            def copy_v(v):
                h, vt = v // VT, v % VT
                act.wait_ge(v_turned, v + 1)
                if h >= 2:
                    act.wait_ge(o_made, h - 1)
                half = slice(vt * P, (vt + 1) * P)
                nc.scalar.activation(v_tok[0:META, h % 2, 0, half], bank[5][0:META, SEQ:SEQ + P], ACT.Copy)
                nc.scalar.activation(v_tok[:, h % 2, 1:, half],
                                     bank[5][:, 0:SEQ].rearrange("p (b n) -> p b n", n=P), ACT.Copy).then_inc(v_tok_ready, 1)

            def copy_o(h):
                act.wait_ge(o_made, h + 1)
                o = o_sb[:, VT * h:VT * h + VT, :]
                nc.scalar.activation(o, bank[3][:].rearrange("p (v t) -> p v t", v=VT), ACT.Copy).then_inc(o_copied, 1)
                act.wait_ge(o_copied, h + 1)
                if h >= 1:
                    act.wait_ge(ms_made, h)
                nc.scalar.activation(o_sq[:], o, ACT.Square).then_inc(o_squared, 1)

            def root_ms(part):
                heads = slice(0, 96) if part == 0 else slice(96, P)
                act.wait_ge(ms_made, 3 if part == 0 else 4)
                nc.scalar.activation(rms[heads, :], bank[2][heads, 0:SEQ], ACT.Sqrt,
                                     bias=eps[heads, 1:2]).then_inc(rms_root, 1)

            def round_y(m):
                act.wait_ge(y_step, m + 1)
                nc.scalar.activation(y_hi[:, m, :], y_t[:, m % 2, :], ACT.Copy).then_inc(yhi_ready, 1)

            for j in range(GLA_TILES):
                gla_tile(j)
                if j == 4:
                    nc.scalar.activation(table_warm[:], eps[:, 0:1], ACT.Exp)
                if j == 5:
                    softplus(0)
                if j == 6:
                    softplus(1)
                if j == 8:
                    nc.scalar.activation(table_warm[:], eps[:, 0:1], ACT.Exp)
                if j == 9:
                    copy_b(0)
                    copy_b(1)
                if j in (10, 11):
                    copy_b(j - 8)
                if 10 <= j < 10 + KD:
                    copy_v(j - 10)
                if j in (9, 11, 13, 15):
                    decays((j - 9) // 2)
                if j in (13, 15, 17, 19):
                    copy_o((j - 13) // 2)
                if j in (18, 20):
                    root_ms((j - 18) // 2)
                for m in Y_CHUNKS.get(j, ()):
                    round_y(m)
            split_hi(n0 + GLA_TILES - 1 + RING)
            out_projection(GLA_NORM, n0 + GLA_TILES, 1, SEQ)

            ffn(3, unit0["f3"], SEQ)

        @block.vector
        def _(dve):
            def split_lo(n, step=0):
                dve.wait_ge(hi_split, step * RING + (n + 1))
                s = n % RING
                nc.vector.tensor_tensor(w_lo[:, s, :], raw[:, s, :], w_hi[:, s, :].bitcast(F32),
                                        ALU.subtract).then_inc(lo_split, 1)

            def take_shift(q, mo, n_tok, step=0):
                r = resid[:, bass.ds(step * 2 + mo, 1), tokens(n_tok)]
                nc.vector.tensor_tensor(r, r, shift[:, tokens(n_tok)], ALU.subtract).then_inc(shift_off, 1)

            def z_chunk(q, mo, n_tok, step=0):
                cols = tokens(n_tok)
                scale = 0.5 if q in FFN_NORM else 1.0
                z = resid[:, bass.ds(step * 2 + mo, 1), cols]
                if mo == 0:
                    if q == 0:
                        dve.wait_ge(alpha_applied, 1)
                    else:
                        dve.wait_ge(resid_ready, KD // 2 * q)
                        dve.wait_ge(resid_late, KD // 2 * q)
                if mo == 1:
                    dve.wait_ge(shift_meaned, q + 1)
                    nc.vector.tensor_copy(shift[:, cols], bank[4][:, 0:n_tok]).then_inc(shift_copied, 1)
                    dve.wait_ge(shift_copied, q + 1)
                    nc.vector.tensor_tensor(resid[:, 0:1, cols], resid[:, 0:1, cols], shift[:, cols],
                                            ALU.subtract).then_inc(shifted, 1)
                    take_shift(q, 1, n_tok)
                if mo >= 1:
                    dve.wait_ge(shift_off, step * 2 + ((KD - 1) * q + mo))
                nc.vector.scalar_tensor_tensor(out=z, in0=bank[6 + mo % 2][:, 0:n_tok], scalar=scale, in1=z,
                                               op0=ALU.mult, op1=ALU.add).then_inc(z_ready, 1)
                if 1 <= mo < KD - 1:
                    take_shift(q, mo + 1, n_tok, step)

            def normalise(q, n_tok, late):
                cols = tokens(n_tok)
                dve.wait_ge(z_ready, KD * (q + 1))
                dve.wait_ge(total_ready, (KD - 2) * (q + 1))
                nc.vector.tensor_tensor(total[:, cols], total[:, cols], resid[:, KD - 1, cols], ALU.add).then_inc(z_summed, 1)
                dve.wait_ge(sq_ready, KD * (q + 1))
                dve.wait_ge(totals_ready, (KD - 2) * (q + 1))
                nc.vector.tensor_tensor(total_sq[:, cols], total_sq[:, cols], sq[:, (KD - 1) % 2, cols],
                                        ALU.add).then_inc(sq_summed, 1)

                def x_low(k):
                    dve.wait_ge(h_ready, KD * q + k + 1)
                    nc.vector.tensor_tensor(x_lo[:, k, cols], h_f[:, k % 3, cols], x_hi[:, k, cols].bitcast(F32),
                                            ALU.subtract).then_inc(xlo_ready, 1)

                dve.wait_ge(stat_ready, 2 * q + 2)
                dve.wait_ge(meansq_ready, q + 1)
                nc.vector.tensor_tensor(var[:, cols], bank[5][:, 0:n_tok], mean_sq[:, cols], ALU.subtract).then_inc(var_ready, 1)
                dve.wait_ge(mean_copied, q + 1)
                nc.vector.tensor_tensor(resid[:, 0, cols], resid[:, 0, cols], mean[:, cols],
                                        ALU.subtract).then_inc(first_centred, 1)
                dve.wait_ge(std_ready, q + 1)
                nc.vector.reciprocal(rstd[:, cols], std[:, cols]).then_inc(rstd_ready, 1)
                dve.wait_ge(rstd_ready, q + 1)
                for k in range(KD):
                    if k == 0:
                        dve.wait_ge(first_centred, q + 1)
                    else:
                        dve.wait_ge(centred, (KD - 1) * q + k)
                    if k >= 3:
                        dve.wait_ge(h_ready, KD * q + k - 2)
                    nc.vector.scalar_tensor_tensor(out=scaled[:, k % 3, cols], in0=resid[:, k, cols],
                                                   scalar=ln_gain_col(q, k), in1=rstd[:, cols], op0=ALU.mult,
                                                   op1=ALU.mult).then_inc(scaled_ready, 1)
                    if k >= 1 and q != LAST_NORM:
                        x_low(k - 1)
                if q == LAST_NORM:
                    for part in range(3):
                        dve.wait_ge(out_turned, part // 2 + 1)
                        nc.vector.tensor_copy(out_tok[:, part % 2, part // 2 * D // 2:(part // 2 + 1) * D // 2],
                                              bank[part][:]).then_inc(out_copied, 1)
                else:
                    x_low(KD - 1)
                for n in late:
                    split_lo(n + RING)

            def out_projection(q, n0, parts, n_tok):
                def chunk(mo, step=0):
                    n = n0 + parts * mo
                    if mo == KD - 1:
                        if parts == 3 and n + RING < UNITS:
                            split_lo(n + RING)
                        dve.wait_ge(unit_used, n + parts)
                        z_chunk(q, mo, n_tok)
                        normalise(q, n_tok, range(n + parts // 2, n + parts) if q != LAST_NORM else ())
                        return
                    for u in range(parts - 1):
                        if n + u + RING < UNITS:
                            split_lo(n + u + RING, step)
                    dve.wait_ge(unit_used, step * RING + (n + parts))
                    z_chunk(q, mo, n_tok, step)
                    if n + parts - 1 + RING < UNITS:
                        split_lo(n + parts - 1 + RING, step)
                if parts == 3:
                    chunk(0)
                    chunk(1)
                    with dve.Fori(0, (KD - 4) // 2) as i:
                        chunk(2, i)
                        chunk(3, i)
                    chunk(KD - 2)
                    chunk(KD - 1)
                else:
                    for mo in range(KD):
                        chunk(mo)

            def ffn(f, n0, n_tok):
                cols = tokens(n_tok)

                def gate_times_up(t, step=0):
                    g = KF * f + t
                    s = t % SETS
                    dve.wait_ge(silu_ready, step * SETS + (g + 1))
                    dve.wait_ge(unit_used, step * RING + (n0 + 2 * t + 2))
                    nc.vector.tensor_tensor(prod[:, s, cols], bank[2 * s + 1][:, 0:n_tok], silu_g[:, s, cols],
                                            ALU.mult).then_inc(prod_ready, 1)
                    dve.wait_ge(prod_ready, step * SETS + (g + 1))
                    at_t = bass.ds(step * SETS + t, 1)
                    nc.vector.tensor_copy(mid_hi[:, at_t, cols], prod[:, s:s + 1, cols]).then_inc(midhi_ready, 1)
                    dve.wait_ge(midhi_ready, step * SETS + (g + 1))
                    nc.vector.tensor_tensor(mid_lo[:, at_t, cols], prod[:, s:s + 1, cols],
                                            mid_hi[:, at_t, cols].bitcast(F32), ALU.subtract).then_inc(mid_ready, 1)

                def tile(t, step=0):
                    n = n0 + 2 * t
                    split_lo(n + RING, step)
                    gate_times_up(t, step)
                    split_lo(n + 1 + RING, step)

                gate_times_up(0)
                split_lo(n0 + RING)
                gate_times_up(1)
                for u in range(1, 4):
                    split_lo(n0 + u + RING)
                with dve.Fori(0, (KF - 4) // SETS) as i:
                    for t in range(2, 2 + SETS):
                        tile(t, i)
                tile(KF - 2)
                tile(KF - 1)
                out_projection(FFN_NORM[f], n0 + FFN_IN, 3, n_tok)

            nc.vector.memset(meanD[:], 1.0 / D)
            nc.vector.memset(meanV[:], 1.0 / HV)
            nc.vector.memset(rstd[:, 0:P], 1.0 / P).then_inc(mean_filled, 1)
            dve.wait_ge(mean_filled, 1)
            nc.vector.tensor_copy(mean128[:], rstd[:, 0:P])
            nc.vector.memset(eps[:, 0:1], LN_EPS)
            nc.vector.memset(gzT[:], 1.0).then_inc(gz_ones, 1)
            nc.vector.memset(eps[:, 1:2], RMS_EPS).then_inc(fills_done, 1)
            def take_x(k):
                dve.wait_ge(x_turned, k + 1)
                nc.vector.tensor_copy(resid[:, k, :], bank[k][:, 0:T]).then_inc(h0_ready, 1)

            def first_x_low(k):
                dve.wait_ge(xhi_ready, k + 1)
                nc.vector.tensor_tensor(x_lo[:, k, :], resid[:, k, :], x_hi[:, k, :].bitcast(F32),
                                        ALU.subtract).then_inc(xlo_ready, 1)

            for k in range(4):
                take_x(k)
            for k in range(4):
                first_x_low(k)
                take_x(k + 4)
            for k in range(4, KD):
                first_x_low(k)
            dve.wait_ge(lo_split, 2)
            for n in range(2, RING):
                split_lo(n)
            dve.wait_ge(consts_ready, 1)

            ffn(0, unit0["f0"], T)

            n0 = unit0["conv"]
            nc.vector.memset(cu[:, :, 0:TAPS - 1], 0.0).then_inc(pad_zeroed, 1)
            dve.wait_ge(pad_zeroed, 1)

            def convolve(m, step=0):
                s = m % 2
                done = 6 * m
                dve.wait_ge(u_copied, step * 2 + (m + 1))
                c_ps, b_ps = bank[3 * s][:, 0:T], bank[3 * s + 2][:, 0:T]
                mm = step * 2 + m
                at_m = bass.ds(mm, 1)
                t0, t1 = conv_t[:, 0:1, :], conv_t[:, 1:2, :]
                nc.vector.tensor_tensor(cu[:, s, TAPS - 1:TAPS - 1 + T], c_ps, u_sb[:, s, :], ALU.mult).then_inc(conv_step, 1)
                dve.wait_ge(conv_step, step * 12 + (done + 1))
                nc.vector.tensor_scalar(t0, cu[:, s:s + 1, 0:T], conv_col(0, mm), None, ALU.mult).then_inc(conv_step, 1)
                dve.wait_ge(conv_step, step * 12 + (done + 2))
                nc.vector.scalar_tensor_tensor(out=t1, in0=cu[:, s:s + 1, 1:1 + T], scalar=conv_col(1, mm), in1=t0,
                                               op0=ALU.mult, op1=ALU.add).then_inc(conv_step, 1)
                dve.wait_ge(conv_step, step * 12 + (done + 3))
                nc.vector.scalar_tensor_tensor(out=t0, in0=cu[:, s:s + 1, 2:2 + T], scalar=conv_col(2, mm), in1=t1,
                                               op0=ALU.mult, op1=ALU.add).then_inc(conv_step, 1)
                split_lo(n0 + 3 * m + 1 + RING, step)
                dve.wait_ge(conv_step, step * 12 + (done + 4))
                dve.wait_ge(unit_used, step * RING + (n0 + 3 * m + 3))
                nc.vector.tensor_tensor(t1, b_ps, t0, ALU.mult).then_inc(conv_step, 1)
                dve.wait_ge(conv_step, step * 12 + (done + 5))
                nc.vector.tensor_copy(yc_hi[:, at_m, :], t1).then_inc(conv_step, 1)
                dve.wait_ge(conv_step, step * 12 + (done + 6))
                nc.vector.tensor_tensor(yc_lo[:, at_m, :], t1, yc_hi[:, at_m, :].bitcast(F32),
                                        ALU.subtract).then_inc(yc_ready, 1)

            def conv_chunk(m, step=0):
                n = n0 + 3 * m
                split_lo(n + RING, step)
                convolve(m, step)
                split_lo(n + 2 + RING, step)

            conv_chunk(0)
            conv_chunk(1)
            with dve.Fori(0, KD // 2 - 1) as i:
                conv_chunk(2, i)
                conv_chunk(3, i)
            out_projection(CONV_NORM, n0 + 3 * KD, 1, T)

            ffn(1, unit0["f1"], T)
            ffn(2, unit0["f2"], T)

            n0 = unit0["gla"]

            def copy_logits():
                for b in range(BLOCKS):
                    r = slice(0, META if b == 0 else P)
                    dve.wait_ge(logits_made, b + 1)
                    nc.vector.tensor_copy(log_a[r, b, :], bank[4 + b][r, :]).then_inc(logits_copied, 1)
                    dve.wait_ge(logits_copied, b + 1)
                    nc.vector.scalar_tensor_tensor(out=soft[r, b, :], in0=log_a[r, b, :], scalar=-1.0, in1=log_a[r, b, :],
                                                   op0=ALU.mult, op1=ALU.min).then_inc(logits_folded, 1)

            def log_sigmoid():
                dve.wait_ge(soft_step, 4)
                for a, s in [(log_a[0:META, 0, :], soft[0:META, 0, :]), (log_a[:, 1:, :], soft[:, 1:, :])]:
                    nc.vector.scalar_tensor_tensor(out=a, in0=a, scalar=0.0, in1=s, op0=ALU.min,
                                                   op1=ALU.subtract).then_inc(log_a_ready, 1)

            def differences(h):
                s = h % 3
                dve.wait_ge(b_copied, h + 1)
                if h >= 2:
                    dve.wait_ge(exps_ready, 5 * (h - 1))
                b_main = b_sb[:, s, META:T].rearrange("p (c i) -> p c i", i=CH)
                b_ref = b_main[:, :, CH // 2:CH // 2 + 1].broadcast_to([P, NC, CH])
                nc.vector.tensor_tensor(d_ref[:, s, :].rearrange("p (c i) -> p c i", i=CH), b_main, b_ref,
                                        ALU.subtract).then_inc(diffs_ready, 1)
                nc.vector.tensor_tensor(d_last[:, h % 2, META:KT0].rearrange("p (c i) -> p c i", i=CH),
                                        b_main[:, 0:NC - 1, :], b_main[:, 0:NC - 1, CH - 1:CH].broadcast_to([P, NC - 1, CH]),
                                        ALU.subtract).then_inc(diffs_ready, 1)
                nc.vector.tensor_tensor(d_last[:, h % 2, 0:META], b_sb[:, s, 0:META],
                                        b_sb[:, s, META - 1:META].broadcast_to([P, META]), ALU.subtract).then_inc(diffs_ready, 1)

            def copy_k(h):
                dve.wait_ge(k_turned, h + 1)
                for b in range(BLOCKS):
                    r = slice(0, META if b == 0 else P if b < BLOCKS - 1 else CH)
                    last = nc.vector.tensor_copy(k_tok[r, h % 2, b, :], bank[4][r, b * P:(b + 1) * P])
                last.then_inc(k_tok_ready, 1)

            def copy_scores(h):
                dve.wait_ge(scores_made, h + 1)
                if h >= 2:
                    dve.wait_ge(o_made, h - 1)
                nc.vector.tensor_copy(sT[:, h % 2, :], bank[2][:, SEQ:2 * SEQ]).then_inc(scores_copied, 1)

            def states(h):
                dve.wait_ge(outer_made, h + 1)
                if h >= 1:
                    dve.wait_ge(o_made, h)
                dve.wait_ge(exps_ready, 5 * h + 5)
                for c in range(NC):
                    ps = outer_tile(c)
                    if c == 0:
                        nc.vector.tensor_copy(state[:, 0, :], ps).then_inc(state_ready, 1)
                        continue
                    dve.wait_ge(state_ready, NC * h + c)
                    nc.vector.scalar_tensor_tensor(out=state[:, c, :], in0=state[:, c - 1, :],
                                                   scalar=decay[:, h, c:c + 1], in1=ps, op0=ALU.mult,
                                                   op1=ALU.add).then_inc(state_ready, 1)

            def invert_rms(part):
                heads = slice(0, 96) if part == 0 else slice(96, P)
                dve.wait_ge(rms_root, part + 1)
                nc.vector.reciprocal(rms[heads, :], rms[heads, :]).then_inc(rms_ready, 1)

            def scale_o(h):
                dve.wait_ge(rms_spread, h + 1)
                for vt in range(VT):
                    o = o_sb[:, VT * h + vt, :]
                    nc.vector.scalar_tensor_tensor(out=o, in0=o, scalar=norm_col(vt), in1=bank[RMS_BANKS[h]][:, 0:SEQ],
                                                   op0=ALU.mult, op1=ALU.mult).then_inc(o_scaled, 1)

            def y_low(m):
                dve.wait_ge(yhi_ready, m + 1)
                nc.vector.tensor_tensor(y_lo[:, m, :], y_t[:, m % 2, :], y_hi[:, m, :].bitcast(F32),
                                        ALU.subtract).then_inc(y_ready, 1)

            for j in range(GLA_TILES):
                if j < GLA_TILES - 1:
                    split_lo(n0 + j + RING)
                if j == 4:
                    copy_logits()
                if j == 6:
                    log_sigmoid()
                if j in (9, 10, 11, 13):
                    differences((9, 10, 11, 13).index(j))
                if j in (11, 13, 15, 17):
                    copy_k((j - 11) // 2)
                    copy_scores((j - 11) // 2)
                if j in (12, 14, 16, 18):
                    states((j - 12) // 2)
                if j == 18:
                    invert_rms(0)
                if j in (19, 20):
                    scale_o(j - 19)
                if j == 20:
                    invert_rms(1)
                if j == 21:
                    scale_o(2)
                if j == 22:
                    scale_o(3)
                for m in Y_CHUNKS.get(j, ()):
                    y_low(m)
            split_lo(n0 + GLA_TILES - 1 + RING)
            out_projection(GLA_NORM, n0 + GLA_TILES, 1, SEQ)

            ffn(3, unit0["f3"], SEQ)

        @block.tensor
        def _(pe):
            def block_of(w, n, k):
                return w[:, n % RING, k * P:(k + 1) * P]

            def multiply(ps, n, source, cols, k0=0, k1=KU, first=True, last=True, step=0, ready=None):
                hi, lo = source
                pe.wait_ge(lo_split, step * RING + (n + 1))
                for k in range(k0, k1):
                    if ready is not None:
                        pe.wait_ge(ready[0], ready[1] + k + 1)
                    w_h, w_l = block_of(w_hi, n, k - k0), block_of(w_lo, n, k - k0)
                    nc.tensor.matmul(ps, w_h, hi[:, k, cols], start=first and k == k0, stop=False)
                    nc.tensor.matmul(ps, w_h, lo[:, k, cols], start=False, stop=False)
                    mm = nc.tensor.matmul(ps, w_l, hi[:, k, cols], start=False, stop=last and k == k1 - 1)
                mm.then_inc(unit_used, 1)

            def multiply_together(outs, n0, q):
                cols = tokens(outs[0].shape[-1])
                gen = q + 1
                for u in range(len(outs)):
                    pe.wait_ge(lo_split, n0 + u + 1)
                keep_warm(n0, WARM[1])
                pe.wait_ge(var_ready, q + 1)
                keep_warm(n0, WARM[2])
                pe.wait_ge(std_ready, q + 1)
                keep_warm(n0, WARM[3])
                for k in range(KD):
                    pe.wait_ge(xhi_ready, KD * gen + k + 1)
                    for u, ps in enumerate(outs):
                        nc.tensor.matmul(ps, block_of(w_hi, n0 + u, k), x_hi[:, k, cols], start=k == 0, stop=False)
                        nc.tensor.matmul(ps, block_of(w_lo, n0 + u, k), x_hi[:, k, cols], start=False, stop=False)
                    pe.wait_ge(xlo_ready, KD * gen + k + 1)
                    for u, ps in enumerate(outs):
                        mm = nc.tensor.matmul(ps, block_of(w_hi, n0 + u, k), x_lo[:, k, cols], start=False,
                                              stop=k == KD - 1)
                        if k == KD - 1:
                            mm.then_inc(unit_used, 1)

            def keep_warm(n, count, free=bank[6]):
                for _ in range(count):
                    nc.tensor.matmul(free[:], block_of(w_hi, n, 0), w_hi[:, n % RING, 0:512], start=True, stop=True)

            def statistics(q, n_tok, n_next):
                cols = tokens(n_tok)
                if n_next < UNITS:
                    pe.wait_ge(lo_split, n_next + 1)
                    pe.wait_ge(z_ready, KD * (q + 1) - 1)
                    keep_warm(n_next, WARM[0])
                pe.wait_ge(z_summed, q + 1)
                nc.tensor.matmul(bank[4][:, 0:n_tok], meanD[:], total[:, cols], start=True, stop=True).then_inc(stat_ready, 1)
                pe.wait_ge(sq_summed, q + 1)
                nc.tensor.matmul(bank[5][:, 0:n_tok], meanD[:], total_sq[:, cols], start=True, stop=True).then_inc(stat_ready, 1)

            def out_projection(q, n0, k_parts, source, ready, n_tok):
                shift_in = 0 if source[0].shape[2] == T else T - n_tok
                src_cols = slice(tokens(n_tok).start - shift_in, T - shift_in)
                cols = tokens(n_tok)
                parts = len(k_parts)

                def mean_of_first():
                    pe.wait_ge(z0_rounded, q + 1)
                    nc.tensor.matmul(bank[4][:, 0:n_tok], mean128[:], z0_hi[:, cols], start=True,
                                     stop=True).then_inc(shift_meaned, 1)

                def chunk(mo, step=0):
                    ps = bank[6 + mo % 2][:, 0:n_tok]
                    if mo >= 2:
                        pe.wait_ge(z_ready, step * 2 + (KD * q + mo - 1))
                    for u, (k0, k1) in enumerate(k_parts):
                        if mo == 1 and parts == 3 and u == 1:
                            mean_of_first()
                        multiply(ps, n0 + parts * mo + u, source, src_cols, k0, k1, u == 0, u == parts - 1, step,
                                 ready if mo == 0 else None)
                    if mo == 1 and parts == 1:
                        mean_of_first()

                if parts == 3:
                    chunk(0)
                    chunk(1)
                    with pe.Fori(0, (KD - 4) // 2) as i:
                        chunk(2, i)
                        chunk(3, i)
                    chunk(KD - 2)
                    chunk(KD - 1)
                else:
                    for mo in range(KD):
                        chunk(mo)
                statistics(q, n_tok, n0 + parts * KD)

            def ffn(f, n0, n_tok, q):
                cols = tokens(n_tok)

                def tile(t, step=0, ready=None):
                    g = KF * f + t
                    if t >= SETS:
                        pe.wait_ge(mid_ready, step * SETS + (g - SETS + 1))
                    for half in range(2):
                        multiply(bank[2 * (t % SETS) + half][:, 0:n_tok], n0 + 2 * t + half, (x_hi, x_lo), cols,
                                 step=step, ready=ready if half == 0 else None)

                if q is None:
                    tile(0, ready=(xlo_ready, 0))
                    turn_constants()
                    tile(1)
                else:
                    multiply_together([bank[b][:, 0:n_tok] for b in range(4)], n0, q)
                if q is None:
                    pe.wait_ge(consts_ready, 1)
                tile(2)
                tile(3)
                tile(4)
                with pe.Fori(0, (KF - 4) // SETS - 1) as i:
                    for t in range(5, 5 + SETS):
                        tile(t, i)
                tile(KF - 2)
                tile(KF - 1)
                out_projection(FFN_NORM[f], n0 + FFN_IN, K_PARTS, (mid_hi, mid_lo), (mid_ready, KF * f), n_tok)

            def turn_constants():
                n_rows = consts.shape[1]
                pe.wait_ge(rows_landed, 16 * 4)
                pe.wait_ge(xlo_ready, KD)
                nc.tensor.transpose(bank[5][:, 0:n_rows], const_rows[0:n_rows, :],
                                    ident[0:n_rows, 0:n_rows]).then_inc(consts_turned, 1)

            pe.wait_ge(masks_set, 1)
            pe.wait_ge(meta_landed, 16)
            for k in range(KD):
                if k == KD // 2:
                    pe.wait_ge(hi_split, 1)
                    keep_warm(0, 2, bank[KD - 1])
                if k % (KD // 2) == 0:
                    pe.wait_ge(x_landed[k // (KD // 2)], 16)
                chunk_cols = slice(k * P, (k + 1) * P)
                nc.tensor.transpose(bank[k][:, 0:META], meta_tok[:, chunk_cols], ident[0:META, 0:META])
                for b in range(SEQ // P):
                    mm = nc.tensor.transpose(bank[k][:, META + b * P:META + (b + 1) * P], x_tok[:, b, chunk_cols], ident[:])
                mm.then_inc(x_turned, 1)
            pe.wait_ge(fills_done, 1)

            ffn(0, unit0["f0"], T, None)

            n0 = unit0["conv"]
            every = slice(0, T)
            multiply_together([bank[b][:, 0:T] for b in range(4)], n0, FFN_NORM[0])

            def conv_chunk(m, step=0):
                if m >= 2:
                    pe.wait_ge(yc_ready, step * 2 + (m - 1))
                for part in range(1 if m == 1 else 0, 3):
                    multiply(bank[3 * (m % 2) + part][:, 0:T], n0 + 3 * m + part, (x_hi, x_lo), every, step=step)

            conv_chunk(1)
            with pe.Fori(0, KD // 2 - 1) as i:
                conv_chunk(2, i)
                conv_chunk(3, i)
            out_projection(CONV_NORM, n0 + 3 * KD, [(0, KU)], (yc_hi, yc_lo), (yc_ready, 0), T)

            ffn(1, unit0["f1"], T, CONV_NORM)
            ffn(2, unit0["f2"], T, FFN_NORM[1])

            n0 = unit0["gla"]
            main = tokens(SEQ)

            def logits():
                pe.wait_ge(gla_evac, 1)
                pe.wait_ge(gate_landed, 32)
                for b in range(BLOCKS):
                    r = slice(0, META) if b == 0 else slice(META + (b - 1) * P, META + b * P)
                    nc.tensor.matmul(bank[4 + b][0:r.stop - r.start, :], gzT[:, r], gate_up[:], start=True,
                                     stop=True).then_inc(logits_made, 1)

            def cumulate(h):
                pe.wait_ge(log_a_ready, 2)
                pe.wait_ge(masks_set, 3)
                if h >= 2:
                    pe.wait_ge(b_copied, h - 1)
                for b in range(BLOCKS):
                    r = slice(0, META) if b == 0 else slice(META + (b - 1) * P, META + b * P)
                    size = r.stop - r.start
                    mm = nc.tensor.matmul(bank[6 + h % 2][:, r], log_a[0:size, b, h * P:(h + 1) * P],
                                          cum[0:size, 0:size], start=True, stop=True)
                mm.then_inc(cum_made, 1)

            def turn_v(v):
                pe.wait_ge(gla_evac, 2 + 2 * HEADS + v)
                if v >= 1:
                    pe.wait_ge(v_tok_ready, v)
                nc.tensor.transpose(bank[5][0:META, SEQ:SEQ + P], vT[:, v % 2, span(0)], ident[:])
                for b in range(SEQ // P):
                    mm = nc.tensor.transpose(bank[5][:, b * P:(b + 1) * P], vT[:, v % 2, META + b * P:META + (b + 1) * P], ident[:])
                mm.then_inc(v_turned, 1)

            def turn_k(h):
                pe.wait_ge(kst_ready, h + 1)
                if h >= 1:
                    pe.wait_ge(state_ready, NC * h)
                for b in range(BLOCKS):
                    r = slice(0, META) if b == 0 else slice(META + (b - 1) * P, min(META + b * P, KT0))
                    mm = nc.tensor.transpose(bank[4][0:r.stop - r.start, b * P:(b + 1) * P], k_st[:, h % 2, r], ident[:])
                mm.then_inc(k_turned, 1)

            def scores(h):
                pe.wait_ge(decayed, 2 * h + 2)
                for b in range(SEQ // P):
                    i = slice(b * P, (b + 1) * P)
                    mm = nc.tensor.matmul(bank[2][:, SEQ + b * P:SEQ + (b + 1) * P], kT[:, h, META + b * P:META + (b + 1) * P], q_pos[:, h, i],
                                          start=True, stop=True)
                mm.then_inc(scores_made, 1)

            def outers(h):
                pe.wait_ge(k_tok_ready, h + 1)
                pe.wait_ge(v_tok_ready, VT * (h + 1))
                if h >= 1:
                    pe.wait_ge(state_ready, NC * h)
                else:
                    pe.wait_ge(b_copied, HEADS)
                for c in range(NC):
                    mm = nc.tensor.matmul(outer_tile(c), k_tok[rows(c), h % 2, blk(c), :],
                                          v_tok[rows(c), h % 2, blk(c), :], start=True, stop=True)
                mm.then_inc(outer_made, 1)

            def outputs(h):
                pe.wait_ge(scores_masked, 2 * h + 2)
                pe.wait_ge(state_ready, NC * (h + 1))
                if h:
                    pe.wait_ge(o_copied, h)
                for vt in range(VT):
                    v_cols = slice(vt * P, (vt + 1) * P)
                    for b in range(SEQ // P):
                        first = vt * SEQ + b * P
                        nc.tensor.matmul(bank[3][:, first:first + P], v_tok[:, h % 2, 1 + b, v_cols],
                                         sT[:, h % 2, b * P:(b + 1) * P], start=True, stop=False)
                        for c in (2 * b + 1, 2 * b + 2):
                            ps = bank[3][:, vt * SEQ + (c - 1) * CH:vt * SEQ + c * CH]
                            mm = nc.tensor.matmul(ps, state[:, c - 1, v_cols], qT[:, h, body(c)], start=False,
                                                  stop=c == 2 * b + 2)
                mm.then_inc(o_made, 1)

            def mean_square(h):
                pe.wait_ge(o_squared, h + 1)
                pe.wait_ge(scores_copied, min(h + 2, HEADS))
                for vt in range(VT):
                    mm = nc.tensor.matmul(bank[2][32 * h:32 * h + 32, 0:SEQ], meanV[:, 0:32], o_sq[:, vt, :],
                                          start=vt == 0, stop=vt == VT - 1)
                mm.then_inc(ms_made, 1)

            def spread_rms(h):
                pe.wait_ge(rms_ready, 1 if h < 3 else 2)
                pe.wait_ge(masks_set, 3 + HEADS)
                pe.wait_ge(state_ready, NC * HEADS)
                rows32 = slice(32 * h, 32 * h + 32)
                nc.tensor.matmul(bank[RMS_BANKS[h]][:, 0:SEQ], pick[rows32, :], rms[rows32, :], start=True,
                                 stop=True).then_inc(rms_spread, 1)

            multiply_together([bank[b][:, 0:T] for b in range(4)], n0, FFN_NORM[2])
            for j in range(4, GLA_TILES):
                pe.wait_ge(gla_evac, j - 3 if j < 6 else j - 1)
                short = HEADS < j <= 2 * HEADS or j > 2 * HEADS + KD
                cols = main if short else every
                multiply(bank[j % 2][:, 0:SEQ if short else T], n0 + j, (x_hi, x_lo), cols)
                if j == 4:
                    logits()
                if j == 9:
                    cumulate(0)
                    cumulate(1)
                if j in (10, 11):
                    cumulate(j - 8)
                if 10 <= j < 10 + KD:
                    turn_v(j - 10)
                if j in (13, 15, 17, 19):
                    outputs((j - 13) // 2)
                if j in (11, 13, 15, 17):
                    turn_k((j - 11) // 2)
                    scores((j - 11) // 2)
                if j in (12, 14, 16, 18):
                    outers((j - 12) // 2)
                if j in (14, 16, 18, 20):
                    mean_square((j - 14) // 2)
                if j in (19, 20):
                    spread_rms(j - 19)
                if j == 20:
                    spread_rms(2)
                if j == 22:
                    spread_rms(3)
            out_projection(GLA_NORM, n0 + GLA_TILES, [(0, KU)], (y_hi, y_lo), (y_ready, 0), SEQ)

            ffn(3, unit0["f3"], SEQ, GLA_NORM)

            for k in range(KD):
                pe.wait_ge(h_ready, KD * LAST_NORM + k + 1)
                for b in range(SEQ // P):
                    mm = nc.tensor.transpose(bank[2 * (k // (KD // 2)) + b][:, (k % (KD // 2)) * P:(k % (KD // 2) + 1) * P],
                                             resid[:, k, META + b * P:META + (b + 1) * P], ident[:])
                if k % (KD // 2) == KD // 2 - 1:
                    mm.then_inc(out_turned, 1)


_INS = ["x", "meta_tokens", "ln_gain", "ln_bias", "ffn_w_in", "ffn_w_out", "conv_w_in", "conv_w", "conv_w_out",
        "gla_w_in", "gla_w_gate_up", "gla_b_gate", "gla_norm_w", "gla_w_out"]
_OUTS = [((1, 256, 1024), "float32")]


def kernel(**inputs):
    import numpy as _np
    import concourse.bacc as _bacc
    from concourse import mybir as _mybir
    from concourse.bass_utils import run_bass_kernel_spmd as _run

    nc = _bacc.Bacc("TRN2", target_bir_lowering=False, num_devices=1)
    arrays, args = {}, []
    for name in _INS:
        a = _np.ascontiguousarray(inputs[name])
        arrays[f"in_{name}_dram"] = a
        args.append(nc.dram_tensor(f"in_{name}_dram", a.shape, _mybir.dt.from_np(a.dtype), kind="ExternalInput").ap())
    for i, (shape, dtype) in enumerate(_OUTS):
        dt = _mybir.dt.from_np(_np.dtype(dtype))
        args.append(nc.dram_tensor(f"out_{i}_dram", shape, dt, kind="ExternalOutput").ap())
    hybrid_trunk(nc, *args)
    r = _run(nc, [arrays], core_ids=[0])
    got = tuple(r.results[0][f"out_{i}_dram"] for i in range(len(_OUTS)))
    return got[0]
```
